# Optimizing a Trainium2 kernel written in Bass

```python
import math
import jax, jax.numpy as jnp
from jax import lax
import numpy as np

D_MODEL = 1024
BATCH = 1
SEQ = 512
DEPTH = 2

RW_HEADS = 8
RW_HEAD_DIM = 64
RW_W = RW_HEADS * RW_HEAD_DIM
DECAY_LORA = 64
ICLR_LORA = 64
GATE_LORA = 128
LNX_EPS = 64e-5
RW_COLS = 3 * RW_W + DECAY_LORA + ICLR_LORA + GATE_LORA
POOL_GROUPS = 4
POOL_W = 512
POOL_GW = POOL_W // POOL_GROUPS
POOL_WINDOWS = (2, 4, 8, 16)
POOL_MAXW = 16
CONV_W = 512
CONV_K = 3
ATT_HQ = 8
ATT_HKV = 2
ATT_G = ATT_HQ // ATT_HKV
ATT_HD = 64
ATT_WINDOW = 128
ATT_BLOCK = 128
ROPE_THETA = 10000.0
ATT_COLS = (ATT_HQ + 2 * ATT_HKV) * ATT_HD
N_BRANCH = 4
GATE_COLS = N_BRANCH * D_MODEL
IN_COLS = RW_COLS + POOL_W + 3 * CONV_W + ATT_COLS + GATE_COLS
IN_SPLITS = (RW_COLS, RW_COLS + POOL_W, RW_COLS + POOL_W + 3 * CONV_W, RW_COLS + POOL_W + 3 * CONV_W + ATT_COLS)
D_FF = ((8 * D_MODEL // 3 + 255) // 256) * 256
NORM_EPS = 1e-6

kernel_name = 'hybrid_gated_parallel_block'

def rms_norm(x, g):
    xf = x.astype(jnp.float32)
    y = xf * lax.rsqrt(jnp.mean(xf * xf, axis=-1, keepdims=True) + NORM_EPS)
    return (y * g.astype(jnp.float32)).astype(x.dtype)

def token_shift(u):
    return jnp.pad(u, ((0, 0), (1, 0), (0, 0)))[:, :-1]

def wkv7_scan(r, decay, k, v, kk, a):
    b, s, h, n = r.shape

    def step(state, inp):
        r_t, w_t, k_t, v_t, kk_t, a_t = inp
        s_kk = jnp.einsum('bhij,bhj->bhi', state, kk_t)
        state = (state * w_t[:, :, None, :]
                 - s_kk[..., None] * (kk_t * a_t)[:, :, None, :]
                 + v_t[..., None] * k_t[:, :, None, :])
        y_t = jnp.einsum('bhij,bhj->bhi', state, r_t)
        return state, y_t

    xs = tuple(jnp.moveaxis(t, 1, 0) for t in (r, decay, k, v, kk, a))
    state0 = jnp.zeros((b, h, n, n), jnp.float32)
    _, ys = lax.scan(step, state0, xs)
    return jnp.moveaxis(ys, 0, 1)

def rwkv7_mixer(p, mu, w_decay_up, w0, a_up, a0, g_up, k_k, k_a, r_k, lnx_g, lnx_b):
    dt = p.dtype
    b, s, _ = p.shape
    p = p.astype(jnp.float32)
    p = p + (token_shift(p) - p) * mu.astype(jnp.float32)
    r, k, v, wd, ad, gd = jnp.split(
        p, [RW_W, 2 * RW_W, 3 * RW_W, 3 * RW_W + DECAY_LORA, 3 * RW_W + DECAY_LORA + ICLR_LORA], axis=-1)
    w = -jax.nn.softplus(-(w0 + jnp.tanh(wd) @ w_decay_up)) - 0.5
    decay = jnp.exp(-jnp.exp(w))
    a = jax.nn.sigmoid(a0 + ad @ a_up)
    g = jax.nn.sigmoid(gd) @ g_up
    heads = lambda t: t.reshape(b, s, RW_HEADS, RW_HEAD_DIM)
    kk = heads(k * k_k)
    kk = kk / jnp.maximum(jnp.sqrt(jnp.sum(kk * kk, axis=-1, keepdims=True)), 1e-12)
    k = k * (1.0 + (a - 1.0) * k_a)
    rh, kh, vh, ah = heads(r), heads(k), heads(v), heads(a)
    y = wkv7_scan(rh, heads(decay), kh, vh, kk, ah)
    mean = jnp.mean(y, axis=-1, keepdims=True)
    var = jnp.mean(jnp.square(y - mean), axis=-1, keepdims=True)
    y = ((y - mean) * lax.rsqrt(var + LNX_EPS)).reshape(b, s, RW_W) * lnx_g + lnx_b
    bonus = jnp.sum(rh * kh * r_k.astype(jnp.float32), axis=-1, keepdims=True) * vh
    y = y + bonus.reshape(b, s, RW_W)
    return (y * g).astype(dt)

def pool_mixer(u, pool_w, pool_scale):
    dt = u.dtype
    b, s, _ = u.shape
    uf = u.astype(jnp.float32)
    cs = jnp.cumsum(uf, axis=1)
    cs_pad = jnp.pad(cs, ((0, 0), (POOL_MAXW, 0), (0, 0)))
    t = jnp.arange(s)
    outs = []
    for gi, win in enumerate(POOL_WINDOWS):
        sl = slice(gi * POOL_GW, (gi + 1) * POOL_GW)
        lag = cs_pad[:, POOL_MAXW - win:POOL_MAXW - win + s, sl]
        count = jnp.minimum(t + 1, win).astype(jnp.float32)[None, :, None]
        outs.append((cs[..., sl] - lag) / count - uf[..., sl])
    z = jnp.stack(outs, axis=2)
    z = jnp.einsum('bsgc,gcd->bsgd', z, pool_w.astype(jnp.float32)).reshape(b, s, POOL_W)
    return (z * pool_scale.astype(jnp.float32)).astype(dt)

def causal_depthwise_conv(u, w):
    c = u.shape[-1]
    return lax.conv_general_dilated(
        u, w[:, None, :].astype(u.dtype), window_strides=(1,), padding=[(CONV_K - 1, 0)],
        dimension_numbers=('NWC', 'WIO', 'NWC'), feature_group_count=c)

def short_conv_mixer(p, conv_w):
    b_gate, c_gate, u = jnp.split(p, [CONV_W, 2 * CONV_W], axis=-1)
    return b_gate * causal_depthwise_conv(c_gate * u, conv_w)

def rope(x, positions):
    half = x.shape[-1] // 2
    inv = ROPE_THETA ** (-jnp.arange(half, dtype=jnp.float32) * 2.0 / x.shape[-1])
    ang = positions.astype(jnp.float32)[..., None] * inv
    cos, sin = jnp.cos(ang)[:, :, None, :], jnp.sin(ang)[:, :, None, :]
    x1, x2 = x[..., :half], x[..., half:]
    return jnp.concatenate([x1 * cos - x2 * sin, x2 * cos + x1 * sin], axis=-1)

def swa_sink_attention(p, positions, q_norm_g, k_norm_g, sinks):
    dt = p.dtype
    b, s, _ = p.shape
    q, k, v = jnp.split(p, [ATT_HQ * ATT_HD, (ATT_HQ + ATT_HKV) * ATT_HD], axis=-1)
    q = rope(rms_norm(q.reshape(b, s, ATT_HQ, ATT_HD), q_norm_g).astype(jnp.float32), positions)
    k = rope(rms_norm(k.reshape(b, s, ATT_HKV, ATT_HD), k_norm_g).astype(jnp.float32), positions)
    v = v.reshape(b, s, ATT_HKV, ATT_HD).astype(jnp.float32)
    nb = s // ATT_BLOCK
    qb = q.reshape(b, nb, ATT_BLOCK, ATT_HKV, ATT_G, ATT_HD)

    def with_prev(t):
        t = t.reshape(b, nb, ATT_BLOCK, ATT_HKV, ATT_HD)
        prev = jnp.pad(t, ((0, 0), (1, 0), (0, 0), (0, 0), (0, 0)))[:, :-1]
        return jnp.concatenate([prev, t], axis=2)

    kc, vc = with_prev(k), with_prev(v)
    scores = jnp.einsum('bnqkgd,bnjkd->bnkgqj', qb, kc) * (ATT_HD ** -0.5)
    qi = jnp.arange(ATT_BLOCK)[:, None] + ATT_BLOCK
    kj = jnp.arange(2 * ATT_BLOCK)[None, :]
    dist = qi - kj
    band = (dist >= 0) & (dist < ATT_WINDOW)
    has_prev = (jnp.arange(nb)[:, None, None] > 0) | (kj >= ATT_BLOCK)[None]
    mask = band[None] & has_prev
    scores = jnp.where(mask[None, :, None, None], scores, -jnp.inf)
    sink = sinks.astype(jnp.float32).reshape(ATT_HKV, ATT_G)[None, None, :, :, None, None]
    m = jnp.maximum(jnp.max(scores, axis=-1, keepdims=True), sink)
    e = jnp.exp(scores - m)
    probs = e / (jnp.sum(e, axis=-1, keepdims=True) + jnp.exp(sink - m))
    o = jnp.einsum('bnkgqj,bnjkd->bnqkgd', probs, vc).reshape(b, s, ATT_HQ * ATT_HD)
    return o.astype(dt)

def setup_inputs(seed: int = 0) -> dict:
    key = jax.random.key(seed)
    ks = jax.random.split(key, 32)
    f32 = jnp.float32
    nrm = lambda i, shape, scale: jax.random.normal(ks[i], shape, f32) * scale
    L = DEPTH
    x = jax.random.normal(ks[0], (BATCH, SEQ, D_MODEL), f32)
    offset = jax.random.randint(ks[1], (BATCH, 1), 0, 1024, dtype=jnp.int32)
    positions = offset + jnp.arange(SEQ, dtype=jnp.int32)[None, :]
    return {
        'x': x,
        'positions': positions,
        'norm1_g': 1.0 + nrm(2, (L, D_MODEL), 0.02),
        'w_in': nrm(3, (L, D_MODEL, IN_COLS), D_MODEL ** -0.5),
        'shift_mu': jax.random.uniform(ks[4], (L, RW_COLS), f32),
        'w_decay_up': nrm(5, (L, DECAY_LORA, RW_W), 0.1 * DECAY_LORA ** -0.5),
        'w0': jax.random.uniform(ks[6], (L, RW_W), f32, -5.0, -0.5),
        'a_up': nrm(7, (L, ICLR_LORA, RW_W), ICLR_LORA ** -0.5),
        'a0': nrm(8, (L, RW_W), 0.1),
        'g_up': nrm(9, (L, GATE_LORA, RW_W), GATE_LORA ** -0.5),
        'k_k': 0.85 + nrm(10, (L, RW_W), 0.05),
        'k_a': 1.0 + nrm(11, (L, RW_W), 0.05),
        'r_k': nrm(12, (L, RW_HEADS, RW_HEAD_DIM), 0.1),
        'lnx_g': 1.0 + nrm(13, (L, RW_W), 0.02),
        'lnx_b': nrm(14, (L, RW_W), 0.02),
        'w_rwkv_out': nrm(15, (L, RW_W, D_MODEL), RW_W ** -0.5),
        'pool_w': nrm(16, (L, POOL_GROUPS, POOL_GW, POOL_GW), POOL_GW ** -0.5),
        'pool_scale': 1.0 + nrm(17, (L, POOL_W), 0.1),
        'w_pool_out': nrm(18, (L, POOL_W, D_MODEL), POOL_W ** -0.5),
        'conv_w': nrm(19, (L, CONV_K, CONV_W), CONV_K ** -0.5),
        'w_conv_out': nrm(20, (L, CONV_W, D_MODEL), CONV_W ** -0.5),
        'q_norm_g': 1.0 + nrm(21, (L, ATT_HD), 0.02),
        'k_norm_g': 1.0 + nrm(22, (L, ATT_HD), 0.02),
        'sinks': nrm(23, (L, ATT_HQ), 1.0),
        'w_attn_out': nrm(24, (L, ATT_HQ * ATT_HD, D_MODEL), (ATT_HQ * ATT_HD) ** -0.5),
        'w_o': nrm(25, (L, D_MODEL, D_MODEL), D_MODEL ** -0.5),
        'norm2_g': 1.0 + nrm(26, (L, D_MODEL), 0.02),
        'w_ffn_gate': nrm(27, (L, D_MODEL, D_FF), D_MODEL ** -0.5),
        'w_ffn_up': nrm(28, (L, D_MODEL, D_FF), D_MODEL ** -0.5),
        'w_ffn_down': nrm(29, (L, D_FF, D_MODEL), D_FF ** -0.5),
    }

def reference(x, positions, norm1_g, w_in, shift_mu, w_decay_up, w0, a_up, a0, g_up, k_k, k_a, r_k,
              lnx_g, lnx_b, w_rwkv_out, pool_w, pool_scale, w_pool_out, conv_w, w_conv_out,
              q_norm_g, k_norm_g, sinks, w_attn_out, w_o, norm2_g, w_ffn_gate, w_ffn_up, w_ffn_down):
    b, s, d = x.shape
    for i in range(DEPTH):
        h = rms_norm(x, norm1_g[i])
        p = h @ w_in[i]
        p_rw, p_pool, p_conv, p_att, p_gate = jnp.split(p, IN_SPLITS, axis=-1)
        y_a = rwkv7_mixer(p_rw, shift_mu[i], w_decay_up[i], w0[i], a_up[i], a0[i], g_up[i],
                          k_k[i], k_a[i], r_k[i], lnx_g[i], lnx_b[i]) @ w_rwkv_out[i]
        y_b = pool_mixer(p_pool, pool_w[i], pool_scale[i]) @ w_pool_out[i]
        y_c = short_conv_mixer(p_conv, conv_w[i]) @ w_conv_out[i]
        y_d = swa_sink_attention(p_att, positions, q_norm_g[i], k_norm_g[i], sinks[i]) @ w_attn_out[i]
        gates = jax.nn.sigmoid(p_gate.astype(jnp.float32)).reshape(b, s, N_BRANCH, d).astype(x.dtype)
        mixed = (gates[:, :, 0] * y_a + gates[:, :, 1] * y_b
                 + gates[:, :, 2] * y_c + gates[:, :, 3] * y_d)
        x = x + mixed @ w_o[i]
        h = rms_norm(x, norm2_g[i])
        x = x + (jax.nn.silu(h @ w_ffn_gate[i]) * (h @ w_ffn_up[i])) @ w_ffn_down[i]
    return x


_drawn_inputs = setup_inputs


def setup_inputs(seed=0):
    import zlib

    import numpy as np

    out = dict(_drawn_inputs(seed))
    spreads = {}
    factors = {'w_decay_up': 8.0,
     'a0': 4.375,
     'k_k': 4.438,
     'k_a': 2.799,
     'lnx_g': 7.569,
     'lnx_b': 7.903,
     'q_norm_g': 8.0,
     'k_norm_g': 8.0,
     'sinks': 64.0,
     'norm2_g': 3.194}
    for name, (base, spread) in spreads.items():
        noise = np.random.default_rng([zlib.crc32(name.encode()), seed]).standard_normal(out[name].shape)
        drawn = base * np.exp(spread * noise) if base else spread * noise
        out[name] = __import__('jax').numpy.asarray(drawn.astype(out[name].dtype))
    for name, factor in factors.items():
        out[name] = (out[name] * factor).astype(out[name].dtype)
    return out
```

```python
from contextlib import ExitStack
import math

import concourse.bass as bass
from concourse import mybir

F32 = mybir.dt.float32
F32R = mybir.dt.float32r
I32 = mybir.dt.int32
U8 = mybir.dt.uint8
ACT = mybir.ActivationFunctionType
ALU = mybir.AluOpType
AX = mybir.AxisListType.X

LAYERS = 2
SEQ = 512
D_MODEL = 1024
KT = D_MODEL // 128
RW_W = 512
IN_COLS = 8704
IN_TILES = IN_COLS // 128
CONV_T0 = (1792 + 512) // 128
POOL_T0 = 1792 // 128
ATT_T0 = (1792 + 512 + 1536) // 128
GATE_T0 = ATT_T0 + 768 // 128
CONV_K = 3
POOL_WINDOWS = (2, 4, 8, 16)
HEADS = 8
WINDOW = 128
CHUNK = 64
D_FF = 2816
FT = D_FF // 128
NORM_EPS = 1e-6
LNX_EPS = 64e-5
ROPE_THETA = 10000.0
MASKED = -1e30
TT = SEQ // 128

CB = 4
RING = 4
BRANCH_ORDER = (2, 1, 3, 0)
PROJ_TILES = GATE_T0
C_PROJ = PROJ_TILES * KT // CB
C_GROUP = (KT + 4) // CB
C_BRANCH = KT * C_GROUP
C_BEFORE_RWKV = C_PROJ + 3 * C_BRANCH
C_WO = C_BEFORE_RWKV + C_BRANCH
C_FFN = C_WO + KT * KT // CB
C_DOWN = C_FFN + 2 * FT * KT // CB
CHUNKS = C_DOWN + KT * FT // CB
BLOCKS = CHUNKS * CB
assert all(c % RING == 0 for c in (C_PROJ, C_BRANCH, C_BEFORE_RWKV, C_WO, C_FFN, C_DOWN, CHUNKS))

ACCS = 4
T_RW = 14
T_CONV = T_RW
T_POOL = T_CONV + 12
T_ATT = T_POOL + 4
T_MIX = PROJ_TILES
T_MIX_A = T_MIX + 2 * KT * 3
T_WO = T_MIX_A + 2 * KT
T_FFN = T_WO + KT
T_DOWN = T_FFN + 2 * FT

_c = 0
COL = {}
for _n, _w in (("norm1", 8), ("norm2", 8), ("mu", 14), ("w0", 4), ("a0", 4), ("k_k", 4), ("k_a", 4), ("r_k", 4),
               ("lnx_g", 4), ("lnx_b", 4), ("pool_scale", 4), ("conv_w", 12), ("q_g", 1), ("k_g", 1), ("sinks", 8),
               ("lora_up", 512), ("g_up", 512), ("pool_w", 512)):
    COL[_n] = _c
    _c += _w
PARAM_COLS = _c
_c = 0
CON = {}
for _n, _w in (("eye", 128), ("same_head", 128), ("ones", 128), ("rot", 128), ("eye2", 64), ("corr", 64),
               ("bias_first", 256), ("bias", 256), ("inv_freq", 1)):
    CON[_n] = _c
    _c += _w
CONST_COLS = _c
_c = 0
MSK = {}
for _n, _w in (("upper", 128), ("upper_eq", 128), ("pair", 128), ("pair_t", 128), ("levels", 5 * 128), ("scan", SEQ)):
    MSK[_n] = _c
    _c += _w
MASK_COLS = _c


def hybrid_gated_parallel_block(nc, x_dram, pos_dram, w_dram, params_dram, consts_dram, masks_dram, out_dram):
    DECAY = math.exp(-0.5)
    scratch = nc.dram_tensor("scratch", (7, TT, 128, 4, 128), F32, kind="Internal").ap()
    SA, SR, SB, SK, SV, SG, SBON = range(7)

    with ExitStack() as ctx:
        at = [(nc.sbuf_base + 63) // 64 * 64]

        def place(name, shape, dt, offset=None):
            size = mybir.dt.size(dt)
            for n in shape[1:]:
                size *= n
            if offset is None:
                offset = at[0]
                at[0] += (size + 63) // 64 * 64
            assert offset + size <= nc.sbuf_usable_end, (name, offset + size)
            return nc.alloc_sbuf_tensor_at(name, list(shape), dt, offset=offset)

        xT = place("xT", [128, KT, SEQ], F32)
        consts = place("consts", [128, CONST_COLS], F32)
        masks = place("masks", [128, MASK_COLS], U8)
        params = place("params", [128, PARAM_COLS], F32)
        cosT = place("cosT", [128, SEQ], F32)
        sinT = place("sinT", [128, SEQ], F32)
        raw = place("raw", [128, RING, CB * 128], F32)
        w_hi = place("w_hi", [128, RING, CB * 128], F32R)
        w_lo = place("w_lo", [128, RING, CB * 128], F32R)
        h_hi = place("h_hi", [128, KT, SEQ], F32R)
        h_lo = place("h_lo", [128, KT, SEQ], F32R)
        mixed = place("mixed", [128, KT, SEQ], F32)
        state = place("state", [128, 2, 4, 64], F32)
        wc = place("wc", [128, 4, 8], F32)
        wcl = place("wcl", [128, 4, 2], F32)
        stat = place("stat", [128, 64], F32)
        one_minus_ka = place("one_minus_ka", [128, 4], F32)
        U = at[0]
        KB = 1024
        workA = place("workA", [128, 24, 512], F32, U)
        y3_hi = place("y3_hi", [128, 3, 4, SEQ], F32R, U + 48 * KB)
        y3_lo = place("y3_lo", [128, 3, 4, SEQ], F32R, U + 72 * KB)
        ya_hi = place("ya_hi", [128, 4, SEQ], F32R, U)
        ya_lo = place("ya_lo", [128, 4, SEQ], F32R, U + 8 * KB)
        workR = place("workR", [128, 40, 512], F32, U + 16 * KB)
        mx_hi = place("mx_hi", [128, KT, SEQ], F32R, U + 16 * KB)
        mx_lo = place("mx_lo", [128, KT, SEQ], F32R, U + 32 * KB)
        tmpN = place("tmpN", [128, 5, 512], F32, U + 48 * KB)
        hid_hi = place("hid_hi", [128, FT, SEQ], F32R, U)
        hid_lo = place("hid_lo", [128, FT, SEQ], F32R, U + 44 * KB)
        tmpF = place("tmpF", [128, 4, 512], F32, U + 88 * KB)

        acc = [ctx.enter_context(nc.psum_tensor(f"acc{i}", [128, 512], F32)) for i in range(ACCS)]
        aux = [ctx.enter_context(nc.psum_tensor(f"aux{i}", [128, 512], F32)) for i in range(4)]

        def con(name, w=None):
            c = CON[name]
            return consts[:, c:c + (w or 128)]

        def msk(name, i=0, w=128):
            c = MSK[name] + i * w
            return masks[:, c:c + w]

        def par(name, i=0):
            c = COL[name] + i
            return params[:, c:c + 1]

        def mat(name, i=0):
            c = COL[name] + 128 * i
            return params[:, c:c + 128]

        def W(i, n=512, off=0):
            return workA[:, :, :].rearrange("p s n -> p (s n)")[:, i * 512 + off:i * 512 + off + n]

        def R(i, n=512):
            return workR[:, :, :].rearrange("p s n -> p (s n)")[:, i * 512:i * 512 + n]

        def sems(names):
            made = {n: ctx.enter_context(nc.semaphore(n)) for n in names.split()}
            nums = [s.num for s in made.values()]
            assert max(nums) - min(nums) == len(nums) - 1
            return made, range(min(nums), max(nums) + 1)

        setup, _ = sems("const_loaded x_loaded pos_loaded out_stored setup_step angle_ready")
        L, layer_sems = sems(
            "param_loaded raw0 raw1 raw2 raw3 split_hi split_ready chunk_done acc_free "
            "sq1 ssq1 var1 root1 hf1 hh1 h1 sq2 ssq2 var2 root2 hf2 hh2 h2 "
            "vstep astep praw_ready lora_in_ready lora_done sig_done g_done L_ready Lprev_ready E_done "
            "kksq_ready kkssq_done kk_clamped kk_root rk_ready rk_done staged "
            "st_A st_R st_B st_K st_V st_G st_bonus "
            "cs_ready y_full y_hi_ready y_ready pool_raw pool_mm qraw_ready qsq_ready qssq_done qvar_ready "
            "qroot_ready qn_ready rot_done qk_ready v_turned v_ready vpad_ready "
            "scores_done scores_read negmax_ready exp_done probs_ready turned pt_a pt_v pv_done yd_hi_ready yd_ready "
            "gate_sig mixed_ready mx_hi_ready mx_ready sig_ffn hid_full hid_hi_ready hid_ready")
        S, scan_sems = sems(
            "in_AR in_B in_K in_V in_GB zeroed turned4 tokA_ready tokB_ready tokK_ready tokV_ready "
            "gramB gramB_ready gramT base_ready gramK gramK_ready tkv_done tkv_ready "
            "lx lx_ready lm lm_ready ma_done nma_ready blk_ready blk2_ready reff_mm reff_ready pt_mm pt_ready q_mm q_ready wcl_ready "
            "s_mm s_ready y_mm y_read mean_mm yc_ready var_mm yvar yroot yout_ready ya_hi_ready rstep")

        class Step:

            def __init__(self, eng, sem):
                self.eng, self.sem, self.n = eng, sem, 0

            def __call__(self, ins, by=1):
                ins.then_inc(self.sem, by)
                self.n += by
                self.eng.wait_ge(self.sem, self.n)

        def last_chunk(tile):
            if tile < PROJ_TILES:
                return 2 * tile + 2
            if tile < T_WO:
                g, second = divmod(tile - T_MIX, 2)
                return C_PROJ + C_GROUP * g + 2 + second
            if tile < T_FFN:
                return C_WO + 2 * (tile - T_WO) + 2
            if tile < T_DOWN:
                return C_FFN + 2 * (tile - T_FFN) + 2
            return C_DOWN + -(-(tile - T_DOWN + 1) * FT // CB)

        with nc.Block() as block:
            @block.sync
            def _(sp):
                sp.dma_start(consts[:, :], consts_dram).then_inc(setup["const_loaded"], 16)
                sp.dma_start(W(6, MASK_COLS), masks_dram).then_inc(setup["const_loaded"], 16)
                sp.dma_start(xT[:, :, :], x_dram).then_inc(setup["x_loaded"], 16)
                sp.dma_start(W(0).bitcast(I32), pos_dram.rearrange("a s -> (a s)").partition_broadcast(128))\
                    .then_inc(setup["pos_loaded"], 16)
                sp.wait_ge(setup["x_loaded"], 16)

            @block.vector
            def _(dve):
                step = Step(dve, setup["setup_step"])
                dve.wait_ge(setup["const_loaded"], 32)
                step(dve.tensor_copy(masks[:, :], W(6, MASK_COLS)))
                dve.wait_ge(setup["pos_loaded"], 16)
                step(dve.tensor_copy(W(1), W(0).bitcast(I32)))
                step(dve.tensor_scalar(W(2), W(1), consts[:, CON["inv_freq"]:CON["inv_freq"] + 1], None, ALU.mult))
                c1 = 6.28125
                c2 = float(int((2 * math.pi - c1) * 2 ** 21)) / 2 ** 21
                c3 = 2 * math.pi - c1 - c2
                big = 1.5 * 2.0 ** 23
                for i, shift in ((3, 0.0), (4, 0.25)):
                    step(dve.tensor_scalar(W(5), W(2), 1 / (2 * math.pi), shift, ALU.mult, ALU.add))
                    step(dve.tensor_scalar(W(5), W(5), big, None, ALU.add))
                    step(dve.tensor_scalar(W(5), W(5), -big, None, ALU.add))
                    step(dve.scalar_tensor_tensor(W(i), W(5), -c1, W(2), ALU.mult, ALU.add))
                    step(dve.scalar_tensor_tensor(W(i), W(5), -c2, W(i), ALU.mult, ALU.add))
                    step(dve.scalar_tensor_tensor(W(i), W(5), -c3, W(i), ALU.mult, ALU.add))
                    step(dve.tensor_scalar(W(i), W(i), shift * 2 * math.pi, math.pi, ALU.add, ALU.min))
                    dve.tensor_scalar(W(i), W(i), -math.pi, None, ALU.max).then_inc(setup["angle_ready"], 1)

            @block.scalar
            def _(act):
                act.wait_ge(setup["angle_ready"], 2)
                act.activation(sinT[:, :], W(3), ACT.Sin)
                act.activation(cosT[:, :], W(4), ACT.Sin)

        def norm_act(act, i, sq, rstd, hf):
            for k in range(KT):
                if k >= 2:
                    act.wait_ge(L[f"ssq{i}"], k - 1)
                act.activation(sq[k % 2], xT[:, k, :], ACT.Square).then_inc(L[f"sq{i}"], 1)
            act.wait_ge(L[f"var{i}"], 1)
            act.activation(rstd, rstd, ACT.Sqrt).then_inc(L[f"root{i}"], 1)
            for k in range(KT):
                act.wait_ge(L[f"hf{i}"], k + 1)
                act.activation(h_hi[:, k, :], hf[k % 2], ACT.Copy).then_inc(L[f"hh{i}"], 1)

        def norm_pe(pe, i, sq):
            for k in range(KT):
                pe.wait_ge(L[f"sq{i}"], k + 1)
                pe.matmul(aux[0][:, :], con("ones"), sq[k % 2], start=(k == 0), stop=(k == KT - 1))\
                    .then_inc(L[f"ssq{i}"], 1)

        def norm_dve(dve, step, i, gain, rstd, hf):
            dve.wait_ge(L[f"ssq{i}"], KT)
            dve.tensor_scalar(rstd, aux[0][:, :], 1.0 / D_MODEL, NORM_EPS, ALU.mult, ALU.add).then_inc(L[f"var{i}"], 1)
            dve.wait_ge(L[f"root{i}"], 1)
            step(dve.reciprocal(rstd, rstd))

            def low(k):
                dve.wait_ge(L[f"hh{i}"], k + 1)
                dve.tensor_tensor(h_lo[:, k, :], hf[k % 2], h_hi[:, k, :].bitcast(F32), ALU.subtract)\
                    .then_inc(L[f"h{i}"], 1)

            for k in range(KT):
                if k >= 2:
                    dve.wait_ge(L[f"h{i}"], k - 1)
                dve.scalar_tensor_tensor(hf[k % 2], xT[:, k, :], par(gain, k), rstd, ALU.mult, ALU.mult)\
                    .then_inc(L[f"hf{i}"], 1)
                dve.wait_ge(L[f"hf{i}"], k + 1)
                if k >= 1:
                    low(k - 1)
            low(KT - 1)

        def blocks_pe(pe, bank, first, rhs, chunk0, slot0=0, ready=None):
            for k, (hi, lo) in enumerate(rhs):
                c, b = divmod(first + k, CB)
                slot = (slot0 + c) % RING
                if b == 0 or k == 0:
                    pe.wait_ge(L["split_ready"], chunk0 + (c + 1))
                if ready:
                    pe.wait_ge(ready, k + 1)
                wh, wl = (w[:, slot, b * 128:b * 128 + 128] for w in (w_hi, w_lo))
                pe.matmul(bank[:, :], wh, hi, start=(k == 0), stop=False)
                pe.matmul(bank[:, :], wh, lo, start=False, stop=False)
                mm = pe.matmul(bank[:, :], wl, hi, start=False, stop=(k == len(rhs) - 1))
                if b == CB - 1:
                    mm.then_inc(L["chunk_done"], 1)

        h_rhs = [(h_hi[:, k, :], h_lo[:, k, :]) for k in range(KT)]

        def group_pe(pe, tile, bank0, chunk0, slot0, rhs, free):
            if free:
                pe.wait_ge(L["acc_free"], tile - ACCS + 1)
            blocks_pe(pe, acc[bank0], 0, h_rhs, chunk0, slot0)
            if free:
                pe.wait_ge(L["acc_free"], tile - ACCS + 2)
            blocks_pe(pe, acc[bank0 + 1], KT, rhs, chunk0, slot0)

        def group_act(act, n, tile, bank0, done, sg):
            act.wait_ge(L["chunk_done"], done)
            act.wait_ge(L["acc_free"], tile - 2)
            act.activation(sg, acc[bank0][:, :], ACT.Sigmoid).then_inc(L["gate_sig"], 1)

        def group_dve(dve, n, tile, bank0, done, sg, tmp, out, first):
            dve.wait_ge(L["chunk_done"], done)
            dve.wait_ge(L["gate_sig"], n)
            if not first and not (isinstance(n, int) and n == KT + 1):
                dve.wait_ge(L["mixed_ready"], n - (KT + 1))
            dve.tensor_tensor(out if first else tmp, sg, acc[bank0 + 1][:, :], ALU.mult).then_inc(L["acc_free"], 2)
            if not first:
                dve.wait_ge(L["acc_free"], tile + 2)
                dve.tensor_tensor(out, out, tmp, ALU.add).then_inc(L["mixed_ready"], 1)

        def branch_loop(eng, n0, tile0, chunk0, what, rhs=None, sg=None, tmp=None):
            with eng.Fori(0, 2) as it:
                for g in range(4):
                    tile = it * 8 + (tile0 + 2 * g)
                    chunk = it * (4 * C_GROUP) + (chunk0 + C_GROUP * g)
                    slot0 = (C_GROUP * g) % RING
                    bank0 = 2 * g % ACCS
                    n = it * 4 + (n0 + g + 1)
                    if what == "pe":
                        group_pe(eng, tile, bank0, chunk, slot0, rhs, True)
                    if what == "act":
                        if g >= 0:
                            group_act(eng, n, tile, bank0, chunk + 2, sg[g % 2])
                    if what == "dve":
                        out = mixed[:, bass.ds(it * 4 + g, 1), :].rearrange("p a n -> p (a n)")
                        group_dve(eng, n, tile, bank0, chunk + 3, sg[g % 2], tmp, out, False)

        def load_chunks(sp, layer, c0, c1):
            stream = w_dram.rearrange("l c p n -> (l c) p n")

            def load(c, s, rel):
                if rel is not None:
                    sp.wait_ge(L["split_ready"], rel)
                sp.dma_start(raw[:, s, :], stream[bass.ds(layer * CHUNKS + c, 1)].rearrange("a p n -> (a p) n"))\
                    .then_inc(L[f"raw{s}"], 16)

            if c0 == 0:
                for s in range(RING):
                    load(s, s, None)
                c0 = RING
            with sp.Fori(c0 // RING, c1 // RING) as r:
                for s in range(RING):
                    load(r * RING + s, s, r * RING + (s - RING + 1))

        def split_chunks(pool, c0, c1):
            def split(s, loaded, free, done):
                pool.wait_ge(L[f"raw{s}"], loaded)
                if free is not None:
                    pool.wait_ge(L["chunk_done"], free)
                pool.tensor_tensor(w_hi[:, s, :], raw[:, s, :], con("ones", 1).broadcast_to([128, CB * 128]), ALU.mult).then_inc(L["split_hi"], 1)
                pool.wait_ge(L["split_hi"], done)
                pool.tensor_tensor(w_lo[:, s, :], raw[:, s, :], w_hi[:, s, :].bitcast(F32), ALU.subtract)\
                    .then_inc(L["split_ready"], 1)

            if c0 == 0:
                for s in range(RING):
                    split(s, 16, None, s + 1)
                c0 = RING
            with pool.Fori(c0 // RING, c1 // RING) as r:
                for s in range(RING):
                    split(s, r * 16 + 16, r * RING + (s - RING + 1), r * RING + (s + 1))

        with nc.Fori(0, LAYERS) as layer:
            with nc.Block() as block:
                SQ, RSTD, HF = [W(0), W(1)], W(2), [W(3), W(4)]
                LW, SGD = W(5), W(6)
                r_, k_, v_, d_ = W(7), W(8), W(9), W(10)
                sig_, L_, Lp_ = W(11), W(12), W(13)
                E1, E2, E3 = W(14), W(15), W(16)
                a_, kk_, g_ = W(17), W(18), W(19)
                kksq_, kkn_ = W(0), W(1)
                stA, stB, stK, bonus_, rk_ = W(2), W(3), W(4), W(12), W(13)
                praw = [W(20, 513, 513 * i) for i in range(3)]
                Cs, cu, ct = W(20), W(21, 514), W(23, 500, 12)
                ct = W(23)
                yf = [W(10), W(11)]
                pbuf, q1, q2, zp = W(0, 528), W(5, 528), W(13, 528), [W(15), W(16)]
                qraw = [W(17), W(18), W(6)]
                qsq, qrst = W(19), W(12)
                Qf = [W(2), W(3), W(4), W(7)]
                kA, kB = W(20, 640), W(22, 640)
                vtok = W(8, 640).rearrange("p (s n) -> p s n", s=5)
                probs = [W(0, 1024), W(13, 1024)]
                pT = W(15, 1024)
                sgA, tmpA = [W(17), W(18)], W(19)
                row_order = [12, 13] + [i for j in range(4) for i in (j, 4 + j, 8 + j)]

                @block.sync
                def _(sp):
                    sp.dma_start(params[:, :], params_dram[bass.ds(layer, 1)].rearrange("a p n -> (a p) n"))\
                        .then_inc(L["param_loaded"], 16)
                    load_chunks(sp, layer, 0, C_BEFORE_RWKV + 2 * RING)

                @block.gpsimd
                def _(pool):
                    split_chunks(pool, 0, C_BEFORE_RWKV + RING)

                @block.tensor
                def _(pe):
                    norm_pe(pe, 1, SQ)

                    def proj(tile, ready=None):
                        if tile >= ACCS:
                            pe.wait_ge(L["acc_free"], tile - ACCS + 1)
                        blocks_pe(pe, acc[tile % ACCS], 0, h_rhs, 2 * tile, 2 * tile, ready)

                    def lora(j):
                        if j == 0:
                            pe.wait_ge(L["lora_in_ready"], 2)
                            pe.wait_ge(L["acc_free"], 2)
                            pe.wait_ge(L["var1"], 1)
                        else:
                            pe.wait_ge(L["staged"], 5 * j)
                            pe.wait_ge(L["sig_done"], 2 * j)
                            pe.wait_ge(L["g_done"], j)
                        up = mat("lora_up", j)
                        pe.matmul(aux[0][:, :], up[0:64], LW[0:64], start=True, stop=True).then_inc(L["lora_done"], 1)
                        pe.matmul(aux[1][:, :], up[64:128], LW[64:128], start=True, stop=True)\
                            .then_inc(L["lora_done"], 1)
                        pe.matmul(aux[2][:, :], mat("g_up", j), SGD, start=True, stop=True).then_inc(L["lora_done"], 1)

                    def kk_norm(j):
                        pe.wait_ge(L["kksq_ready"], j + 1)
                        if j >= 1:
                            pe.wait_ge(L["kk_clamped"], j)
                        pe.matmul(aux[3][:, :], con("same_head"), kksq_, start=True, stop=True)\
                            .then_inc(L["kkssq_done"], 1)

                    def rk_sum(j):
                        pe.wait_ge(L["rk_ready"], j + 1)
                        pe.matmul(aux[0][:, :], con("same_head"), rk_, start=True, stop=True).then_inc(L["rk_done"], 1)

                    proj(0, L["h1"])
                    proj(1)
                    for j in range(5):
                        t0 = 2 + 3 * j
                        proj(t0)
                        if j >= 1:
                            kk_norm(j - 1)
                        proj(t0 + 1)
                        proj(t0 + 2)
                        if j >= 1:
                            rk_sum(j - 1)
                        if j < 4:
                            lora(j)
                    for t in range(T_CONV + 3, T_POOL):
                        proj(t)

                    def pool_mm(g):
                        pe.wait_ge(L["acc_free"], T_POOL + g + 1)
                        if g == 0:
                            pe.wait_ge(L["staged"], 20)
                        if g >= 2:
                            pe.wait_ge(L["y_full"], 4 + g - 1)
                        pe.matmul(aux[g % 2][:, :], mat("pool_w", g), zp[g % 2], start=True, stop=True)\
                            .then_inc(L["pool_mm"], 1)

                    def q_ssq(i):
                        pe.wait_ge(L["qsq_ready"], i + 1)
                        pe.matmul(aux[2][:, :], con("same_head"), qsq, start=True, stop=True).then_inc(L["qssq_done"], 1)

                    def q_rot(i):
                        pe.wait_ge(L["qn_ready"], i + 1)
                        if i >= 1:
                            pe.wait_ge(L["qk_ready"], i)
                        pe.matmul(aux[3][:, :], con("rot"), qraw[i % 3], start=True, stop=True).then_inc(L["rot_done"], 1)

                    for g in range(4):
                        proj(T_POOL + g)
                        if g >= 1:
                            pool_mm(g - 1)
                    for i in range(6):
                        proj(T_ATT + i)
                        if i == 0:
                            pool_mm(3)
                        if i >= 1:
                            q_ssq(i - 1)
                        if i >= 2:
                            q_rot(i - 2)
                    q_rot(4)
                    pe.wait_ge(L["qraw_ready"], 6)
                    for b in range(TT):
                        mm = pe.transpose(aux[0][:, b * 128:b * 128 + 128], qraw[5 % 3][:, b * 128:b * 128 + 128],
                                          con("eye"))
                    mm.then_inc(L["v_turned"], 1)

                    def group(n):
                        group_pe(pe, T_MIX + 2 * n, 2 * n % ACCS, C_PROJ + C_GROUP * n, C_GROUP * n % RING,
                                 [(y3_hi[:, n // 8, k, :], y3_lo[:, n // 8, k, :]) for k in range(4)], True)

                    pe.wait_ge(L["v_ready"], 1)
                    pe.wait_ge(L["vpad_ready"], 3)
                    pe.wait_ge(L["qk_ready"], 5)
                    pe.wait_ge(L["y_ready"], 8)
                    for n in range(8):
                        b, jj = divmod(n, 2)
                        if n >= 1:
                            pe.wait_ge(L["yd_ready"], n)
                        for tj in range(2):
                            for pr in range(2):
                                rows = slice(64 * pr, 64 * pr + 64)
                                keys = kA if pr == jj else kB
                                mm = pe.matmul(aux[pr][:, tj * 256:tj * 256 + 256],
                                               Qf[2 * jj + tj][rows, b * 128:b * 128 + 128],
                                               keys[rows, b * 128:b * 128 + 256], start=True, stop=True)
                        mm.then_inc(L["scores_done"], 1)
                        group(2 * n)
                        pe.wait_ge(L["probs_ready"], n + 1)
                        if n >= 1:
                            pe.wait_ge(L["pt_a"], n)
                            pe.wait_ge(L["pt_v"], n)
                        for pr in range(2):
                            for s in range(4):
                                mm = pe.transpose(aux[2 + pr][:, s * 128:s * 128 + 128],
                                                  probs[n % 2][:, pr * 512 + s * 128:pr * 512 + s * 128 + 128],
                                                  con("eye"))
                        mm.then_inc(L["turned"], 1)
                        group(2 * n + 1)
                        pe.wait_ge(L["pt_a"], n + 1)
                        pe.wait_ge(L["pt_v"], n + 1)
                        for pr in range(2):
                            for tj in range(2):
                                for blk in range(2):
                                    src = pr * 512 + tj * 256 + blk * 128
                                    mm = pe.matmul(aux[0][64 * pr:64 * pr + 64, tj * 128:tj * 128 + 128],
                                                   vtok[:, b + blk, 64 * jj:64 * jj + 64], pT[:, src:src + 128],
                                                   start=(blk == 0), stop=(blk == 1))
                        mm.then_inc(L["pv_done"], 1)
                    pe.wait_ge(L["yd_ready"], 8)
                    branch_loop(pe, 16, T_MIX + 32, C_PROJ + 2 * C_BRANCH, "pe",
                                rhs=[(y3_hi[:, 2, k, :], y3_lo[:, 2, k, :]) for k in range(4)])

                @block.scalar
                def _(act):
                    norm_act(act, 1, SQ, RSTD, HF)

                    def done(tile):
                        act.wait_ge(L["chunk_done"], last_chunk(tile))

                    def shift_in(n):
                        done(n)
                        if n == 0:
                            act.wait_ge(L["h1"], KT)
                        if n >= 3:
                            act.wait_ge(L["acc_free"], n - 2)
                        act.activation(praw[n % 3][:, 1:513], acc[n % ACCS][:, :], ACT.Copy)\
                            .then_inc(L["praw_ready"], 1)

                    def store(j):
                        act.wait_ge(L["staged"], 5 * (j + 1))
                        for a, src, name in ((SA, stA, "A"), (SR, r_, "R"), (SB, stB, "B"), (SK, stK, "K"),
                                             (SV, v_, "V"), (SG, g_, "G"), (SBON, bonus_, "bonus")):
                            act.dma_start(scratch[a][:, :, j, :].rearrange("t p n -> p t n"),
                                          src.rearrange("p (t n) -> p t n", t=TT)).then_inc(L[f"st_{name}"], 16)

                    shift_in(0)
                    shift_in(1)
                    act.wait_ge(L["acc_free"], 1)
                    act.activation(LW[0:64], LW[0:64], ACT.Tanh).then_inc(L["lora_in_ready"], 1)
                    act.wait_ge(L["acc_free"], 2)
                    act.activation(SGD, SGD, ACT.Sigmoid).then_inc(L["lora_in_ready"], 1)
                    for j in range(4):
                        if j >= 1:
                            store(j - 1)
                        for i in range(3):
                            shift_in(2 + 3 * j + i)
                        act.wait_ge(L["lora_done"], 3 * j + 1)
                        act.activation(sig_, aux[0][:, :], ACT.Sigmoid, bias=par("w0", j)).then_inc(L["sig_done"], 1)
                        act.wait_ge(L["lora_done"], 3 * j + 2)
                        act.activation(a_, aux[1][:, :], ACT.Sigmoid, bias=par("a0", j)).then_inc(L["sig_done"], 1)
                        act.wait_ge(L["lora_done"], 3 * j + 3)
                        if j >= 1:
                            act.wait_ge(L["st_G"], 16 * j)
                        act.activation(g_, aux[2][:, :], ACT.Copy).then_inc(L["g_done"], 1)
                        act.wait_ge(L["L_ready"], j + 1)
                        act.activation(E1, L_, ACT.Exp, scale=-DECAY).then_inc(L["E_done"], 1)
                        act.activation(E2, L_, ACT.Exp, scale=DECAY).then_inc(L["E_done"], 1)
                        act.wait_ge(L["Lprev_ready"], j + 1)
                        act.activation(E3, Lp_, ACT.Exp, scale=-DECAY).then_inc(L["E_done"], 1)
                        act.wait_ge(L["kk_clamped"], j + 1)
                        act.activation(kkn_, kkn_, ACT.Sqrt).then_inc(L["kk_root"], 1)
                    store(3)

                    def high(i):
                        act.wait_ge(L["y_full"], i + 1)
                        act.activation(y3_hi[:, i // 4, i % 4, :], yf[i % 2], ACT.Copy).then_inc(L["y_hi_ready"], 1)

                    for j in range(4):
                        done(T_CONV + 3 * j)
                        act.wait_ge(L["acc_free"], T_CONV + (3 * j - 1 if j else 0))
                        act.activation(Cs, acc[(T_CONV + 3 * j) % ACCS][:, :], ACT.Copy).then_inc(L["cs_ready"], 1)
                        if j >= 1:
                            high(j - 1)
                    for g in range(4):
                        t = T_POOL + g
                        done(t)
                        act.wait_ge(L["acc_free"], t)
                        act.activation(pbuf[:, 16:528], acc[t % ACCS][:, :], ACT.Copy).then_inc(L["pool_raw"], 1)
                        high(3 + g)
                    for i in range(6):
                        t = T_ATT + i
                        done(t)
                        if i == 0:
                            act.wait_ge(L["acc_free"], t)
                        if i >= 3:
                            act.wait_ge(L["qk_ready"], i - 2)
                        act.activation(qraw[i % 3], acc[t % ACCS][:, :], ACT.Copy).then_inc(L["qraw_ready"], 1)
                        if i == 0:
                            high(7)
                        if i >= 1:
                            act.wait_ge(L["qvar_ready"], i)
                            act.activation(qrst, qrst, ACT.Sqrt).then_inc(L["qroot_ready"], 1)
                    act.wait_ge(L["v_turned"], 1)
                    act.wait_ge(L["st_V"], 64)
                    act.activation(vtok[:, 1:5, :], aux[0][:, :].rearrange("p (s n) -> p s n", s=4), ACT.Copy)\
                        .then_inc(L["v_ready"], 1)

                    def gate(n):
                        t = T_MIX + 2 * n
                        group_act(act, n, t, t % ACCS, last_chunk(t), sgA[n % 2])

                    for n in range(8):
                        b, jj = divmod(n, 2)
                        act.wait_ge(L["negmax_ready"], n + 1)
                        for s in range(4):
                            act.activation(probs[n % 2][:, s * 256:s * 256 + 256], probs[n % 2][:, s * 256:s * 256 + 256],
                                           ACT.Exp, bias=stat[:, 4 + s:5 + s], accum_out=stat[:, 8 + s:9 + s])\
                                .then_inc(L["exp_done"], 1)
                        act.activation(stat[:, 12:16], stat[:, 12:16], ACT.Exp).then_inc(L["exp_done"], 1)
                        gate(2 * n)
                        act.wait_ge(L["turned"], n + 1)
                        if n >= 1:
                            act.wait_ge(L["pv_done"], n)
                        act.activation(pT[:, 0:512], aux[2][:, :], ACT.Copy).then_inc(L["pt_a"], 1)
                        gate(2 * n + 1)
                        act.wait_ge(L["pv_done"], n + 1)
                        act.activation(y3_hi[:, 2, 2 * jj:2 * jj + 2, b * 128:b * 128 + 128],
                                       aux[0][:, 0:256].rearrange("p (t n) -> p t n", t=2), ACT.Copy)\
                            .then_inc(L["yd_hi_ready"], 1)
                    branch_loop(act, 16, T_MIX + 32, C_PROJ + 2 * C_BRANCH, "act", sg=sgA)
                    for name in ("A", "R", "B", "K", "V", "G", "bonus"):
                        act.wait_ge(L[f"st_{name}"], 64)

                @block.vector
                def _(dve):
                    step = Step(dve, L["vstep"])
                    free = Step(dve, L["acc_free"])
                    dve.wait_ge(L["param_loaded"], 16)
                    norm_dve(dve, step, 1, "norm1", RSTD, HF)
                    dve.tensor_scalar(one_minus_ka[:, :], params[:, COL["k_a"]:COL["k_a"] + 4], -1.0, 1.0,
                                      ALU.mult, ALU.add)
                    for p in praw:
                        step(dve.memset(p[:, 0:1], 0.0))

                    def done(tile):
                        dve.wait_ge(L["chunk_done"], last_chunk(tile))

                    def mix(n, out):
                        dve.wait_ge(L["praw_ready"], n + 1)
                        p = praw[n % 3]
                        step(dve.tensor_tensor(d_, p[:, 0:512], p[:, 1:513], ALU.subtract))
                        free(dve.scalar_tensor_tensor(out, d_, par("mu", row_order[n]), p[:, 1:513],
                                                      ALU.mult, ALU.add))

                    mix(0, LW)
                    mix(1, SGD)
                    for j in range(4):
                        if j >= 1:
                            dve.wait_ge(L["st_R"], 16 * j)
                            dve.wait_ge(L["st_V"], 16 * j)
                        for i, out in enumerate((r_, k_, v_)):
                            mix(2 + 3 * j + i, out)
                        dve.wait_ge(L["sig_done"], 2 * j + 1)
                        if j >= 1:
                            dve.wait_ge(L["st_bonus"], 16 * j)
                        dve.tensor_tensor_scan(L_, msk("scan", w=SEQ), sig_, 0.0, ALU.mult, ALU.add)\
                            .then_inc(L["L_ready"], 1)
                        dve.wait_ge(L["L_ready"], j + 1)
                        dve.tensor_tensor(Lp_, L_, sig_, ALU.subtract).then_inc(L["Lprev_ready"], 1)
                        step(dve.tensor_scalar(kk_, k_, par("k_k", j), None, ALU.mult))
                        dve.tensor_tensor(kksq_, kk_, kk_, ALU.mult).then_inc(L["kksq_ready"], 1)
                        dve.wait_ge(L["kkssq_done"], j + 1)
                        dve.tensor_scalar(kkn_, aux[3][:, :], 1e-24, None, ALU.max).then_inc(L["kk_clamped"], 1)
                        dve.wait_ge(L["kk_root"], j + 1)
                        step(dve.reciprocal(kkn_, kkn_))
                        step(dve.tensor_tensor(kk_, kk_, kkn_, ALU.mult))
                        dve.wait_ge(L["sig_done"], 2 * j + 2)
                        if j >= 1:
                            for name in ("A", "B", "K"):
                                dve.wait_ge(L[f"st_{name}"], 16 * j)
                        step(dve.tensor_tensor(stB, kk_, a_, ALU.mult))
                        dve.wait_ge(L["E_done"], 3 * j + 3)
                        dve.tensor_tensor(stB, stB, E2, ALU.mult).then_inc(L["staged"], 1)
                        dve.tensor_tensor(stA, kk_, E3, ALU.mult).then_inc(L["staged"], 1)
                        step(dve.tensor_scalar(a_, a_, par("k_a", j), one_minus_ka[:, j:j + 1], ALU.mult, ALU.add))
                        step(dve.tensor_tensor(k_, k_, a_, ALU.mult))
                        dve.tensor_tensor(stK, k_, E2, ALU.mult).then_inc(L["staged"], 1)
                        dve.scalar_tensor_tensor(rk_, r_, par("r_k", j), k_, ALU.mult, ALU.mult)\
                            .then_inc(L["rk_ready"], 1)
                        dve.wait_ge(L["rk_ready"], j + 1)
                        dve.tensor_tensor(r_, r_, E1, ALU.mult).then_inc(L["staged"], 1)
                        step(dve.tensor_copy(wc[:, j, :], E1.rearrange("p (c n) -> p c n", c=8)[:, :, CHUNK - 1]))
                        dve.wait_ge(L["rk_done"], j + 1)
                        dve.tensor_tensor(bonus_, aux[0][:, :], v_, ALU.mult).then_inc(L["staged"], 1)

                    def low(i):
                        dve.wait_ge(L["y_hi_ready"], i + 1)
                        dve.tensor_tensor(y3_lo[:, i // 4, i % 4, :], yf[i % 2],
                                          y3_hi[:, i // 4, i % 4, :].bitcast(F32), ALU.subtract)\
                            .then_inc(L["y_ready"], 1)

                    step(dve.memset(cu[:, 0:2], 0.0))
                    for j in range(4):
                        t = T_CONV + 3 * j
                        done(t + 1)
                        dve.wait_ge(L["cs_ready"], j + 1)
                        free(dve.tensor_tensor(cu[:, 2:514], Cs, acc[(t + 1) % ACCS][:, :], ALU.mult), 2)
                        step(dve.tensor_scalar(ct, cu[:, 0:512], par("conv_w", j), None, ALU.mult))
                        for tap in (1, 2):
                            step(dve.scalar_tensor_tensor(ct, cu[:, tap:tap + 512], par("conv_w", 4 * tap + j), ct,
                                                          ALU.mult, ALU.add))
                        done(t + 2)
                        if j >= 2:
                            dve.wait_ge(L["y_ready"], j - 1)
                        dve.tensor_tensor(yf[j % 2], ct, acc[(t + 2) % ACCS][:, :], ALU.mult).then_inc(L["y_full"], 1)
                        dve.wait_ge(L["y_full"], j + 1)
                        free(dve.memset(stat[:, 63:64], 0.0))
                        if j >= 1:
                            low(j - 1)

                    step(dve.memset(pbuf[:, 0:16], 0.0))

                    def pool_out(g):
                        dve.wait_ge(L["pool_mm"], g + 1)
                        dve.wait_ge(L["y_ready"], 4 + g - 1)
                        dve.tensor_scalar(yf[g % 2], aux[g % 2][:, :], par("pool_scale", g), None, ALU.mult)\
                            .then_inc(L["y_full"], 1)
                        dve.wait_ge(L["y_full"], 4 + g + 1)

                    for g, win in enumerate(POOL_WINDOWS):
                        dve.wait_ge(L["pool_raw"], g + 1)
                        src, dst, other, w = pbuf, q1, q2, 1
                        while w < win:
                            lo = 2 * w - 1
                            step(dve.tensor_tensor(dst[:, lo:528], src[:, lo:528], src[:, lo - w:528 - w], ALU.add))
                            src, dst, other = dst, other, dst
                            w *= 2
                        step(dve.tensor_tensor(src[:, 16:32], src[:, 16:32], consts[:, CON["corr"] + 16 * g:CON["corr"] + 16 * g + 16],
                                               ALU.mult))
                        if g >= 2:
                            dve.wait_ge(L["pool_mm"], g - 1)
                        free(dve.scalar_tensor_tensor(zp[g % 2], src[:, 16:528], 1.0 / win, pbuf[:, 16:528],
                                                      ALU.mult, ALU.subtract))
                        low(3 + g) if g == 0 else None
                        if g >= 1:
                            pool_out(g - 1)
                            low(3 + g)

                    for name in ("A", "B", "K", "R", "V", "G", "bonus"):
                        dve.wait_ge(L[f"st_{name}"], 64)
                    dve.memset(kA[:, 0:128], 0.0).then_inc(L["vpad_ready"], 1)
                    dve.memset(vtok[:, 0, :], 0.0).then_inc(L["vpad_ready"], 1)

                    def q_root(i):
                        dve.wait_ge(L["qssq_done"], i + 1)
                        dve.tensor_scalar(qrst, aux[2][:, :], 1.0 / 64, NORM_EPS, ALU.mult, ALU.add)\
                            .then_inc(L["qvar_ready"], 1)
                        dve.wait_ge(L["qroot_ready"], i + 1)
                        step(dve.reciprocal(qrst, qrst))
                        dve.scalar_tensor_tensor(qraw[i % 3], qraw[i % 3], par("q_g" if i < 4 else "k_g"), qrst,
                                                 ALU.mult, ALU.mult).then_inc(L["qn_ready"], 1)
                        dve.wait_ge(L["qn_ready"], i + 1)

                    def q_turn(i):
                        out = Qf[i] if i < 4 else kA[:, 128:640]
                        step(dve.tensor_tensor(qsq, qraw[i % 3], cosT[:, :], ALU.mult))
                        dve.wait_ge(L["rot_done"], i + 1)
                        step(dve.tensor_tensor(qrst, aux[3][:, :], sinT[:, :], ALU.mult))
                        dve.tensor_tensor(out, qsq, qrst, ALU.add).then_inc(L["qk_ready"], 1)
                        dve.wait_ge(L["qk_ready"], i + 1)

                    for i in range(7):
                        if i < 6:
                            dve.wait_ge(L["qraw_ready"], i + 1)
                        if i == 0:
                            pool_out(3)
                            low(7)
                        if 1 <= i < 6:
                            q_root(i - 1)
                        if i >= 2:
                            q_turn(i - 2)
                        if i < 5:
                            dve.tensor_tensor(qsq, qraw[i % 3], qraw[i % 3], ALU.mult).then_inc(L["qsq_ready"], 1)
                            dve.wait_ge(L["qsq_ready"], i + 1)
                        if i < 6:
                            free(dve.memset(stat[:, 63:64], 0.0))
                    dve.wait_ge(L["vpad_ready"], 2)
                    step(dve.tensor_copy(kB[0:64, :], kA[64:128, :]))
                    dve.tensor_copy(kB[64:128, :], kA[0:64, :]).then_inc(L["vpad_ready"], 1)

                    def mix_in(n):
                        t = T_MIX + 2 * n
                        group_dve(dve, n + 1, t, t % ACCS, last_chunk(t + 1), sgA[n % 2], tmpA, mixed[:, n % 8, :],
                                  n < 8)

                    sinks = params[:, COL["sinks"]:COL["sinks"] + 8].rearrange("p (j q) -> p q j", q=2)
                    for n in range(8):
                        b, jj = divmod(n, 2)
                        P = probs[n % 2]
                        dve.wait_ge(L["scores_done"], n + 1)
                        if n == 0:
                            dve.wait_ge(L["pool_mm"], 4)
                        bias = con("bias" if b else "bias_first", 256).unsqueeze(1).broadcast_to([128, 2, 256])
                        for pr in range(2):
                            step(dve.scalar_tensor_tensor(
                                P[:, pr * 512:pr * 512 + 512].rearrange("p (t n) -> p t n", t=2),
                                aux[pr][:, :].rearrange("p (t n) -> p t n", t=2), 0.125, bias, ALU.mult, ALU.add))
                        step(dve.tensor_reduce(stat[:, 0:4], P.rearrange("p (h n) -> p h n", h=4), AX, ALU.max))
                        sk = sinks[:, :, 2 * jj:2 * jj + 2]
                        m4 = stat[:, 0:4].rearrange("p (q t) -> p q t", q=2)
                        step(dve.tensor_tensor(m4, m4, sk, ALU.max))
                        step(dve.tensor_tensor(stat[:, 12:16].rearrange("p (q t) -> p q t", q=2), sk, m4, ALU.subtract))
                        dve.tensor_scalar(stat[:, 4:8], stat[:, 0:4], -1.0, None, ALU.mult)\
                            .then_inc(L["negmax_ready"], 1)
                        dve.wait_ge(L["exp_done"], 5 * n + 5)
                        step(dve.tensor_tensor(stat[:, 8:12], stat[:, 8:12], stat[:, 12:16], ALU.add))
                        step(dve.reciprocal(stat[:, 8:12], stat[:, 8:12]))
                        p4 = P.rearrange("p (h n) -> p h n", h=4)
                        dve.tensor_tensor(p4, p4, stat[:, 8:12].unsqueeze(2).broadcast_to([128, 4, 256]), ALU.mult)\
                            .then_inc(L["probs_ready"], 1)
                        mix_in(2 * n)
                        dve.wait_ge(L["turned"], n + 1)
                        if n >= 1:
                            dve.wait_ge(L["pv_done"], n)
                        dve.tensor_copy(pT[:, 512:1024], aux[3][:, :]).then_inc(L["pt_v"], 1)
                        mix_in(2 * n + 1)
                        dve.wait_ge(L["yd_hi_ready"], n + 1)
                        tok = slice(b * 128, b * 128 + 128)
                        dve.tensor_tensor(y3_lo[:, 2, 2 * jj:2 * jj + 2, tok],
                                          aux[0][:, 0:256].rearrange("p (t n) -> p t n", t=2),
                                          y3_hi[:, 2, 2 * jj:2 * jj + 2, tok].bitcast(F32), ALU.subtract)\
                            .then_inc(L["yd_ready"], 1)
                    branch_loop(dve, 16, T_MIX + 32, C_PROJ + 2 * C_BRANCH, "dve", sg=sgA, tmp=tmpA)

            with nc.Block() as block:
                @block.vector
                def _(dve):
                    dve.memset(state[:, 0], 0.0)

            with nc.Fori(0, TT) as tt:
                with nc.Block() as block:
                    GB = R(0, 2048).rearrange("p (g j w t) -> p g j w t", g=2, j=4, w=2)
                    GK = R(4, 2048).rearrange("p (g j w t) -> p g j w t", g=2, j=4, w=2)
                    per_head = lambda i: R(i, 1024).rearrange("p (g j t) -> p g j t", g=2, j=4)
                    M, MT, X, MAin, nMA = (per_head(i) for i in (8, 10, 12, 14, 16))
                    tok = lambda i: R(i).rearrange("p (j g c) -> p j g c", j=4, g=2)
                    Btok, Ktok, Vtok = tok(18), tok(19), tok(20)
                    blk = lambda i: R(i, 1024).rearrange("p (j g c n) -> p j g c n", j=4, g=2, c=2)
                    Bblk, Vblk, nMTblk = blk(21), blk(23), blk(25)
                    AR = R(27, 1024).rearrange("p (j w t) -> p j w t", j=4, w=2)
                    feat = lambda i: R(i).rearrange("p (j t) -> p j t", j=4)
                    Bf, Kf, Vf, gf, bonus = (feat(i) for i in (29, 30, 31, 32, 33))
                    Reff = feat(34)
                    PT, Qs = (R(i).rearrange("p (j c n) -> p j c n", j=4, c=2) for i in (35, 36))
                    yv, y1, y2 = feat(37), feat(38), feat(39)
                    rows = lambda g: slice(64 * g, 64 * g + 64)
                    bank4 = lambda b: b[:, :].rearrange("p (j t) -> p j t", j=4)
                    LEVELS = 5

                    @block.sync
                    def _(sp):
                        def load(a, out, name):
                            sp.dma_start(out, scratch[a][bass.ds(tt, 1)].rearrange("a p j n -> (a p) j n"))\
                                .then_inc(S[name], 16)
                        load(SA, AR[:, :, 0, :], "in_AR")
                        load(SR, AR[:, :, 1, :], "in_AR")
                        load(SB, Bf, "in_B")
                        load(SK, Kf, "in_K")
                        load(SV, Vf, "in_V")
                        load(SG, gf, "in_GB")
                        load(SBON, bonus, "in_GB")

                    @block.gpsimd
                    def _(pool):
                        for t in (Bblk, Vblk, nMTblk):
                            pool.memset(t[0:64, :, :, 1, :], 0.0).then_inc(S["zeroed"], 1)
                            pool.memset(t[64:128, :, :, 0, :], 0.0).then_inc(S["zeroed"], 1)
                        pool.wait_ge(S["zeroed"], 6)
                        pool.wait_ge(S["tokB_ready"], 1)
                        for c in range(2):
                            pool.tensor_copy(Bblk[rows(c), :, :, c, :], Btok[rows(c)]).then_inc(S["blk_ready"], 1)
                        pool.wait_ge(S["tokV_ready"], 1)
                        for c in range(2):
                            pool.tensor_copy(Vblk[rows(c), :, :, c, :], Vtok[rows(c)]).then_inc(S["blk_ready"], 1)
                        pool.wait_ge(S["nma_ready"], 2)
                        for c in range(2):
                            for g in range(2):
                                pool.tensor_copy(nMTblk[rows(c), :, g, c, :], nMA[rows(c), g, :, 64:128])\
                                    .then_inc(S["blk2_ready"], 1)

                    @block.tensor
                    def _(pe):
                        for i, (src, name) in enumerate(((AR[:, :, 0, :], "in_AR"), (Bf, "in_B"), (Kf, "in_K"),
                                                         (Vf, "in_V"))):
                            pe.wait_ge(S[name], 32 if i == 0 else 16)
                            for j in range(4):
                                mm = pe.transpose(bank4(aux[i])[:, j, :], src[:, j, :], con("eye"))
                            mm.then_inc(S["turned4"], 1)
                        free = ("tokA_ready", "tokB_ready", "tokK_ready", "tokV_ready")

                        def gram(src, sem, done):
                            for g in range(2):
                                for i in range(2):
                                    b = 2 * g + i
                                    done(b)
                                    for j in range(2 * i, 2 * i + 2):
                                        mm = pe.matmul(aux[b][:, (j % 2) * 256:(j % 2) * 256 + 256], src[rows(g), j, :],
                                                       AR[rows(g), j, :, :].rearrange("p w t -> p (w t)"),
                                                       start=True, stop=True)
                                    mm.then_inc(S[sem], 1)

                        gram(Bf, "gramB", lambda b: pe.wait_ge(S[free[b]], 1))
                        for g in range(2):
                            pe.wait_ge(S["gramB_ready"], 2 * g + 1)
                            for j in range(4):
                                mm = pe.matmul(bank4(aux[2 * g])[:, j, :], AR[rows(g), j, 0, :], Bf[rows(g), j, :],
                                               start=True, stop=True)
                            mm.then_inc(S["gramT"], 1)
                        pe.wait_ge(S["base_ready"], 2)
                        pe.wait_ge(S["gramB_ready"], 4)
                        gram(Kf, "gramK", lambda b: None)
                        pe.wait_ge(S["gramK_ready"], 4)
                        for g in range(2):
                            for j in range(4):
                                mm = pe.matmul(aux[1][:, (4 * g + j) * 64:(4 * g + j) * 64 + 64], GK[:, g, j, 0, :],
                                               Vtok[:, j, g, :], start=True, stop=True)
                        mm.then_inc(S["tkv_done"], 1)
                        for l in range(LEVELS):
                            for g in range(2):
                                pe.wait_ge(S["base_ready"], 2) if l == 0 else pe.wait_ge(S["lm_ready"], 4 * (l - 1) + 2 * g + 2)
                                for j in range(4):
                                    mm = pe.matmul(bank4(aux[2 * g])[:, j, :], GB[:, g, j, 0, :], M[:, g, j, :],
                                                   start=True, stop=True)
                                mm.then_inc(S["lx"], 1)
                            if l == 0:
                                pe.wait_ge(S["tkv_ready"], 1)
                            for g in range(2):
                                pe.wait_ge(S["lx_ready"], 2 * l + g + 1)
                                if l < LEVELS - 1:
                                    for j in range(4):
                                        pe.matmul(bank4(aux[2 * g])[:, j, :], MT[:, g, j, :], X[:, g, j, :],
                                                  start=True, stop=True)
                                for j in range(4):
                                    mm = pe.matmul(bank4(aux[2 * g + 1])[:, j, :], X[:, g, j, :], MT[:, g, j, :],
                                                   start=True, stop=True)
                                mm.then_inc(S["lm"], 1)
                        for g in range(2):
                            pe.wait_ge(S["lm_ready"], 4 * (LEVELS - 1) + g + 1)
                            for j in range(4):
                                mm = pe.matmul(bank4(aux[2 * g])[:, j, :], MT[:, g, j, :], MAin[:, g, j, :],
                                               start=True, stop=True)
                            mm.then_inc(S["ma_done"], 1)
                        pe.wait_ge(S["nma_ready"], 2)
                        for g in range(2):
                            for j in range(4):
                                mm = pe.matmul(bank4(aux[1])[rows(g), j, :], nMA[:, g, j, 0:64], GB[:, g, j, 1, :],
                                               start=True, stop=True)
                        mm.then_inc(S["reff_mm"], 1)
                        pe.wait_ge(S["blk_ready"], 4)
                        for g in range(2):
                            for j in range(4):
                                mm = pe.matmul(bank4(aux[0])[rows(g), j, :], nMA[:, g, j, 0:64],
                                               Bblk[:, j, g].rearrange("p c n -> p (c n)"), start=True, stop=True)
                        mm.then_inc(S["pt_mm"], 1)
                        pe.wait_ge(S["blk2_ready"], 4)
                        for g in range(2):
                            for j in range(4):
                                pe.matmul(bank4(aux[2])[rows(g), j, :], Ktok[:, j, g, :],
                                          Vblk[:, j, g].rearrange("p c n -> p (c n)"), start=True, stop=False)
                                mm = pe.matmul(bank4(aux[2])[rows(g), j, :], Btok[:, j, g, :],
                                               nMTblk[:, j, g].rearrange("p c n -> p (c n)"), start=False, stop=True)
                        mm.then_inc(S["q_mm"], 1)

                        def advance(c, bank):
                            for g in range(2):
                                for j in range(4):
                                    mm = pe.matmul(bank[rows(g), j * 64:j * 64 + 64], PT[rows(g), j, c, :],
                                                   state[rows(g), c, j, :], start=True, stop=True)
                            mm.then_inc(S["s_mm"], 1)

                        pe.wait_ge(S["pt_ready"], 1)
                        advance(0, aux[0])
                        pe.wait_ge(S["reff_ready"], 1)
                        pe.wait_ge(S["s_ready"], 1)
                        advance(1, aux[1])
                        for g in range(2):
                            for j in range(4):
                                out = bank4(aux[3])[rows(g), j, :]
                                pe.matmul(out, Vtok[:, j, g, :], GK[:, g, j, 1, :], start=True, stop=False)
                                pe.matmul(out, nMA[:, g, j, 64:128], GB[:, g, j, 1, :], start=False, stop=False)
                                for c in range(2):
                                    mm = pe.matmul(bank4(aux[3])[rows(g), j, 64 * c:64 * c + 64], state[rows(g), c, j, :],
                                                   Reff[rows(g), j, 64 * c:64 * c + 64], start=False, stop=(c == 1))
                        mm.then_inc(S["y_mm"], 1)
                        pe.wait_ge(S["y_read"], 1)
                        pe.wait_ge(S["q_ready"], 1)
                        pe.matmul(aux[2][:, :], con("same_head"), yv.rearrange("p j t -> p (j t)"), start=True, stop=True)\
                            .then_inc(S["mean_mm"], 1)
                        pe.wait_ge(S["yc_ready"], 2)
                        pe.matmul(aux[3][:, :], con("same_head"), y1.rearrange("p j t -> p (j t)"), start=True, stop=True)\
                            .then_inc(S["var_mm"], 1)

                    @block.scalar
                    def _(act):
                        act.wait_ge(S["turned4"], 1)
                        act.activation(MAin[:, :, :, 0:64].rearrange("p g j c -> p j g c"),
                                       aux[0][:, :].rearrange("p (j g c) -> p j g c", j=4, g=2), ACT.Copy)\
                            .then_inc(S["tokA_ready"], 1)
                        act.wait_ge(S["turned4"], 3)
                        act.activation(Ktok.rearrange("p j g c -> p (j g c)"), aux[2][:, :], ACT.Copy)\
                            .then_inc(S["tokK_ready"], 1)
                        act.wait_ge(S["tkv_done"], 1)
                        act.activation(MAin[:, :, :, 64:128], aux[1][:, :].rearrange("p (g j c) -> p g j c", g=2, j=4),
                                       ACT.Copy).then_inc(S["tkv_ready"], 1)
                        for g in range(2):
                            act.wait_ge(S["ma_done"], g + 1)
                            act.activation(nMA[:, g], bank4(aux[2 * g]), ACT.Copy, scale=-1.0).then_inc(S["nma_ready"], 1)
                        act.wait_ge(S["y_mm"], 1)
                        act.activation(yv.rearrange("p j t -> p (j t)"), aux[3][:, :], ACT.Copy).then_inc(S["y_read"], 1)
                        act.wait_ge(S["yvar"], 1)
                        act.activation(y1, y1, ACT.Sqrt).then_inc(S["yroot"], 1)
                        act.wait_ge(S["yout_ready"], 1)
                        act.activation(ya_hi[:, :, bass.ds(tt * 128, 128)], yv, ACT.Copy).then_inc(S["ya_hi_ready"], 1)

                    @block.vector
                    def _(dve):
                        step = Step(dve, S["rstep"])
                        dve.wait_ge(S["turned4"], 2)
                        dve.tensor_copy(Btok.rearrange("p j g c -> p (j g c)"), aux[1][:, :]).then_inc(S["tokB_ready"], 1)
                        dve.wait_ge(S["turned4"], 4)
                        dve.tensor_copy(Vtok.rearrange("p j g c -> p (j g c)"), aux[3][:, :]).then_inc(S["tokV_ready"], 1)
                        dve.tensor_copy(wcl[:, :, :], wc[:, :, bass.ds(tt * 2, 2)]).then_inc(S["wcl_ready"], 1)
                        both = masks[:, MSK["upper"]:MSK["upper"] + 256].unsqueeze(1).broadcast_to([128, 2, 256])
                        four = lambda ap: ap.unsqueeze(1).broadcast_to([128, 4, 128])

                        def gram(out, sem, b):
                            g, i = divmod(b, 2)
                            dve.wait_ge(S[sem], b + 1)
                            dve.tensor_tensor(out[:, g, 2 * i:2 * i + 2].rearrange("p j w t -> p j (w t)"),
                                              aux[b][:, :].rearrange("p (j n) -> p j n", j=2), both, ALU.mult)\
                                .then_inc(S[sem + "_ready"], 1)
                            dve.wait_ge(S[sem + "_ready"], b + 1)

                        for b in range(4):
                            gram(GB, "gramB", b)
                        for g in range(2):
                            step(dve.tensor_tensor(MT[:, g], GB[:, g, :, 0, :], four(msk("pair_t")), ALU.mult))
                            step(dve.tensor_tensor(MT[:, g], four(con("eye")), MT[:, g], ALU.subtract))
                            dve.wait_ge(S["gramT"], g + 1)
                            step(dve.tensor_tensor(M[:, g], bank4(aux[2 * g]), four(msk("pair")), ALU.mult))
                            dve.tensor_tensor(M[:, g], four(con("eye")), M[:, g], ALU.subtract).then_inc(S["base_ready"], 1)
                            dve.wait_ge(S["base_ready"], g + 1)
                        for b in range(4):
                            gram(GK, "gramK", b)
                        for l in range(LEVELS):
                            for g in range(2):
                                dve.wait_ge(S["lx"], 2 * l + g + 1)
                                dve.tensor_tensor(X[:, g], bank4(aux[2 * g]), four(msk("levels", l)), ALU.mult)\
                                    .then_inc(S["lx_ready"], 1)
                            for g in range(2):
                                dve.wait_ge(S["lm"], 2 * l + g + 1)
                                if l < LEVELS - 1:
                                    dve.tensor_tensor(M[:, g], M[:, g], bank4(aux[2 * g]), ALU.subtract)\
                                        .then_inc(S["lm_ready"], 1)
                                dve.tensor_tensor(MT[:, g], MT[:, g], bank4(aux[2 * g + 1]), ALU.subtract)\
                                    .then_inc(S["lm_ready"], 1)
                                dve.wait_ge(S["lm_ready"], 4 * l + 2 * g + 2 if l < LEVELS - 1 else 4 * l + g + 1)
                        dve.wait_ge(S["reff_mm"], 1)
                        dve.tensor_tensor(Reff, bank4(aux[1]), AR[:, :, 1, :], ALU.add).then_inc(S["reff_ready"], 1)
                        dve.wait_ge(S["pt_mm"], 1)
                        eye2 = con("eye2", 64).unsqueeze(1).broadcast_to([128, 8, 64])
                        dve.tensor_tensor(PT.rearrange("p j c n -> p (j c) n"),
                                          aux[0][:, :].rearrange("p (a n) -> p a n", a=8), eye2, ALU.add)\
                            .then_inc(S["pt_ready"], 1)
                        dve.wait_ge(S["q_mm"], 1)
                        dve.wait_ge(S["wcl_ready"], 1)
                        w8 = wcl[:, :, :].rearrange("p j c -> p (j c)").unsqueeze(2).broadcast_to([128, 8, 64])
                        dve.tensor_tensor(Qs.rearrange("p j c n -> p (j c) n"),
                                          aux[2][:, :].rearrange("p (a n) -> p a n", a=8), w8, ALU.mult)\
                            .then_inc(S["q_ready"], 1)
                        dve.wait_ge(S["q_ready"], 1)
                        for c in range(2):
                            w4 = wcl[:, :, c].unsqueeze(2).broadcast_to([128, 4, 64])
                            dve.wait_ge(S["s_mm"], c + 1)
                            part = y2.rearrange("p j t -> p (j t)")[:, 256 * c:256 * c + 256].rearrange("p (j n) -> p j n", j=4)
                            step(dve.tensor_tensor(part, aux[c][:, 0:256].rearrange("p (j n) -> p j n", j=4), w4, ALU.mult))
                            if c == 1:
                                dve.wait_ge(S["y_mm"], 1)
                            dve.tensor_tensor(state[:, 1 - c], part, Qs[:, :, c, :], ALU.add).then_inc(S["s_ready"], 1)
                            dve.wait_ge(S["s_ready"], c + 1)
                        lanes = lambda name: params[:, COL[name]:COL[name] + 4].unsqueeze(2).broadcast_to([128, 4, 128])
                        dve.wait_ge(S["mean_mm"], 1)
                        dve.scalar_tensor_tensor(yv, bank4(aux[2]), -1.0 / 64, yv, ALU.mult, ALU.add)\
                            .then_inc(S["yc_ready"], 1)
                        dve.wait_ge(S["yc_ready"], 1)
                        dve.tensor_tensor(y1, yv, yv, ALU.mult).then_inc(S["yc_ready"], 1)
                        step(dve.tensor_tensor(yv, yv, lanes("lnx_g"), ALU.mult))
                        dve.wait_ge(S["var_mm"], 1)
                        dve.tensor_scalar(y1, bank4(aux[3]), 1.0 / 64, LNX_EPS, ALU.mult, ALU.add).then_inc(S["yvar"], 1)
                        dve.wait_ge(S["in_GB"], 32)
                        step(dve.tensor_tensor(bonus, bonus, lanes("lnx_b"), ALU.add))
                        dve.wait_ge(S["yroot"], 1)
                        step(dve.reciprocal(y1, y1))
                        step(dve.tensor_tensor(yv, yv, y1, ALU.mult))
                        step(dve.tensor_tensor(yv, yv, bonus, ALU.add))
                        dve.tensor_tensor(yv, yv, gf, ALU.mult).then_inc(S["yout_ready"], 1)
                        dve.wait_ge(S["ya_hi_ready"], 1)
                        step(dve.tensor_tensor(ya_lo[:, :, bass.ds(tt * 128, 128)], yv,
                                               ya_hi[:, :, bass.ds(tt * 128, 128)].bitcast(F32), ALU.subtract))
                nc.all_engine_barrier(sems_to_clear=scan_sems)

            with nc.Block() as block:
                SQ, RSTD, HF = [tmpN[:, 0, :], tmpN[:, 1, :]], tmpN[:, 2, :], [tmpN[:, 3, :], tmpN[:, 4, :]]
                sgC, tC = [tmpF[:, 0, :], tmpF[:, 1, :]], [tmpF[:, 2, :], tmpF[:, 3, :]]

                @block.sync
                def _(sp):
                    load_chunks(sp, layer, C_BEFORE_RWKV + 2 * RING, CHUNKS)

                @block.gpsimd
                def _(pool):
                    split_chunks(pool, C_BEFORE_RWKV + RING, CHUNKS)

                @block.tensor
                def _(pe):
                    branch_loop(pe, 24, T_MIX_A, C_BEFORE_RWKV, "pe",
                                rhs=[(ya_hi[:, k, :], ya_lo[:, k, :]) for k in range(4)])
                    for m in range(KT):
                        pe.wait_ge(L["acc_free"], T_WO + m - ACCS + 1)
                        blocks_pe(pe, acc[m % ACCS], 0, [(mx_hi[:, k, :], mx_lo[:, k, :]) for k in range(KT)],
                                  C_WO + 2 * m, 2 * m, L["mx_ready"] if m == 0 else None)
                    norm_pe(pe, 2, SQ)
                    pe.wait_ge(L["h2"], KT)
                    with pe.Fori(0, FT // 2) as it:
                        for i in range(4):
                            pe.wait_ge(L["acc_free"], it * 4 + (T_FFN + i - ACCS + 1))
                            blocks_pe(pe, acc[i], 0, h_rhs, it * 8 + (C_FFN + 2 * i), 2 * i)
                    pe.wait_ge(L["hid_ready"], FT)
                    for m in range(KT):
                        pe.wait_ge(L["acc_free"], T_DOWN + m - ACCS + 1)
                        first = m * FT
                        blocks_pe(pe, acc[m % ACCS], first, [(hid_hi[:, k, :], hid_lo[:, k, :]) for k in range(FT)],
                                  C_DOWN, 0)

                @block.scalar
                def _(act):
                    branch_loop(act, 24, T_MIX_A, C_BEFORE_RWKV, "act", sg=sgC)
                    for m in range(KT):
                        if m % 4 == 0:
                            act.wait_ge(L["mixed_ready"], 16 + KT)
                        act.activation(mx_hi[:, m, :], mixed[:, m, :], ACT.Copy).then_inc(L["mx_hi_ready"], 1)
                    act.wait_ge(L["acc_free"], T_FFN)
                    norm_act(act, 2, SQ, RSTD, HF)
                    act.wait_ge(L["h2"], KT)
                    with act.Fori(0, FT // 2) as it:
                        for i in range(2):
                            act.wait_ge(L["chunk_done"], it * 8 + (C_FFN + 4 * i + 2))
                            act.wait_ge(L["acc_free"], it * 4 + (T_FFN + 2 * i))
                            act.activation(sgC[i], acc[2 * i][:, :], ACT.Sigmoid).then_inc(L["sig_ffn"], 1)
                        for i in range(2):
                            act.wait_ge(L["hid_full"], it * 2 + (i + 1))
                            act.activation(hid_hi[:, bass.ds(it * 2 + i, 1), :].rearrange("p a n -> p (a n)"), tC[i],
                                           ACT.Copy).then_inc(L["hid_hi_ready"], 1)

                @block.vector
                def _(dve):
                    step = Step(dve, L["astep"])
                    branch_loop(dve, 24, T_MIX_A, C_BEFORE_RWKV, "dve", sg=sgC, tmp=tC[0])
                    for m in range(KT):
                        dve.wait_ge(L["mx_hi_ready"], m + 1)
                        dve.tensor_tensor(mx_lo[:, m, :], mixed[:, m, :], mx_hi[:, m, :].bitcast(F32), ALU.subtract)\
                            .then_inc(L["mx_ready"], 1)
                    for m in range(KT):
                        dve.wait_ge(L["chunk_done"], last_chunk(T_WO + m))
                        dve.tensor_tensor(xT[:, m, :], xT[:, m, :], acc[m % ACCS][:, :], ALU.add)\
                            .then_inc(L["acc_free"], 1)
                    dve.wait_ge(L["acc_free"], T_FFN)
                    norm_dve(dve, step, 2, "norm2", RSTD, HF)
                    with dve.Fori(0, FT // 2) as it:
                        for i in range(2):
                            dve.wait_ge(L["sig_ffn"], it * 2 + (i + 1))
                            dve.tensor_tensor(tC[i], sgC[i], acc[2 * i][:, :], ALU.mult).then_inc(L["acc_free"], 1)
                            dve.wait_ge(L["acc_free"], it * 4 + (T_FFN + 2 * i + 1))
                            dve.wait_ge(L["chunk_done"], it * 8 + (C_FFN + 4 * i + 4))
                            dve.tensor_tensor(tC[i], tC[i], acc[2 * i + 1][:, :], ALU.mult).then_inc(L["hid_full"], 1)
                            dve.wait_ge(L["hid_full"], it * 2 + (i + 1))
                            dve.memset(stat[:, 63:64], 0.0).then_inc(L["acc_free"], 1)
                        for i in range(2):
                            dve.wait_ge(L["hid_hi_ready"], it * 2 + (i + 1))
                            f = bass.ds(it * 2 + i, 1)
                            dve.tensor_tensor(hid_lo[:, f, :].rearrange("p a n -> p (a n)"), tC[i],
                                              hid_hi[:, f, :].rearrange("p a n -> p (a n)").bitcast(F32), ALU.subtract)\
                                .then_inc(L["hid_ready"], 1)
                        dve.wait_ge(L["hid_ready"], it * 2 + 2)
                    for m in range(KT):
                        dve.wait_ge(L["chunk_done"], last_chunk(T_DOWN + m))
                        dve.tensor_tensor(xT[:, m, :], xT[:, m, :], acc[m % ACCS][:, :], ALU.add)\
                            .then_inc(L["acc_free"], 1)
            nc.all_engine_barrier(sems_to_clear=layer_sems)

        with nc.Block() as block:
            @block.sync
            def _(sp):
                sp.dma_start(out_dram, xT[:, :, :]).then_inc(setup["out_stored"], 16)
                sp.wait_ge(setup["out_stored"], 16)


def tile_blocks(w, rows, cols):
    L = w.shape[0]
    return w.reshape(L, rows, 128, cols, 128).transpose(0, 3, 1, 2, 4)


def weight_stream(inp):
    import numpy as np
    w_in = tile_blocks(inp["w_in"], KT, IN_TILES)
    order = [12, 13] + [i for j in range(4) for i in (j, 4 + j, 8 + j)]
    order += [i for j in range(4) for i in (CONV_T0 + 4 + j, CONV_T0 + 8 + j, CONV_T0 + j)]
    order += [POOL_T0 + g for g in range(4)] + [ATT_T0 + i for i in range(6)]
    parts = [w_in[:, i] for i in order]
    outs = {b: tile_blocks(inp[n], 4, KT) for b, n in enumerate(("w_rwkv_out", "w_pool_out", "w_conv_out", "w_attn_out"))}
    for b in BRANCH_ORDER:
        for m in range(KT):
            parts += [w_in[:, GATE_T0 + KT * b + m], outs[b][:, m]]
    w_o = tile_blocks(inp["w_o"], KT, KT)
    parts += [w_o[:, m] for m in range(KT)]
    gate, up = (tile_blocks(inp[n], KT, FT) for n in ("w_ffn_gate", "w_ffn_up"))
    for f in range(FT):
        parts += [gate[:, f], up[:, f]]
    down = tile_blocks(inp["w_ffn_down"], FT, KT)
    parts += [down[:, m] for m in range(KT)]
    s = np.concatenate(parts, axis=1)
    L, n = s.shape[:2]
    assert n == BLOCKS
    return np.ascontiguousarray(s.reshape(L, n // CB, CB, 128, 128).transpose(0, 1, 3, 2, 4)).reshape(L, n // CB, 128, CB * 128)


def small_params(inp):
    import numpy as np
    L = inp["x"].shape[0] and inp["w_in"].shape[0]
    col = lambda v: v.reshape(L, -1, 128).transpose(0, 2, 1)
    twice = lambda v: np.concatenate([v, v], axis=1).reshape(L, 128, 1)
    cw = inp["conv_w"].reshape(L, CONV_K, 4, 128).transpose(0, 3, 1, 2).reshape(L, 128, CONV_K * 4)
    sinks = np.broadcast_to(inp["sinks"][:, None, :], (L, 128, HEADS))
    parts = [col(inp["norm1_g"]), col(inp["norm2_g"]), col(inp["shift_mu"]), col(inp["w0"]), col(inp["a0"]),
             col(inp["k_k"]), col(inp["k_a"]), col(inp["r_k"].reshape(L, -1)), col(inp["lnx_g"]), col(inp["lnx_b"]),
             col(inp["pool_scale"]), cw, twice(inp["q_norm_g"]), twice(inp["k_norm_g"]), sinks,
             np.concatenate([inp["w_decay_up"], inp["a_up"]], axis=1), inp["g_up"],
             inp["pool_w"].transpose(0, 2, 1, 3).reshape(L, 128, 512)]
    out = np.concatenate(parts, axis=2)
    assert out.shape[2] == PARAM_COLS
    return np.ascontiguousarray(out)


def constants():
    import numpy as np
    p = np.arange(128)
    row, col = p[:, None], p[None, :]
    same = row // CHUNK == col // CHUNK
    eye = (row == col)
    rot = np.where((col % 64 < 32) & (row == col + 32), -1.0, 0.0) + np.where((col % 64 >= 32) & (row == col - 32), 1.0, 0.0)
    eye2 = (row % 64 == np.arange(64)[None, :])
    t = np.arange(16)
    corr = np.concatenate([w / np.minimum(t + 1, w) for w in POOL_WINDOWS])[None, :].repeat(128, 0)
    key = np.arange(256)[None, :]
    dist = row + 128 - key
    band = (dist >= 0) & (dist < WINDOW)
    bias = [np.where(band & (key >= 128), 0.0, MASKED), np.where(band, 0.0, MASKED)]
    inv = (np.float32(ROPE_THETA) ** (-(p % 32).astype(np.float32) * np.float32(2.0) / np.float32(64)))[:, None]
    f = np.concatenate([eye, same, np.ones((128, 128)), rot, eye2, corr, *bias, inv], axis=1).astype(np.float32)
    levels = []
    for b in (2, 4, 8, 16, 32):
        levels.append((row // (2 * b) == col // (2 * b)) & (row // b > col // b))
    pair = (row // 2 == col // 2) & (row > col)
    scan = np.broadcast_to((np.arange(SEQ) % CHUNK != 0)[None, :], (128, SEQ))
    u = np.concatenate([same & (row < col), same & (row <= col), pair, pair.T, *levels, scan], axis=1).astype(np.float32)
    assert f.shape[1] == CONST_COLS and u.shape[1] == MASK_COLS
    return np.ascontiguousarray(f), np.ascontiguousarray(u)


def kernel(**inputs):
    import numpy as _np
    import concourse.bacc as _bacc
    from concourse import mybir as _mybir
    from concourse.bass_utils import run_bass_kernel_spmd as _run

    inp = {k: _np.asarray(v) for k, v in inputs.items()}
    f, u = constants()
    arrays = {
        "x_dram": _np.ascontiguousarray(inp["x"][0].T.reshape(KT, 128, SEQ).transpose(1, 0, 2)),
        "positions_dram": _np.ascontiguousarray(inp["positions"]),
        "weights_dram": weight_stream(inp),
        "params_dram": small_params(inp),
        "consts_dram": f,
        "masks_dram": u,
    }
    nc = _bacc.Bacc("TRN2", target_bir_lowering=False, num_devices=1)
    args = [nc.dram_tensor(n, a.shape, _mybir.dt.from_np(a.dtype), kind="ExternalInput").ap() for n, a in arrays.items()]
    out = nc.dram_tensor("out_dram", (128, KT, SEQ), _mybir.dt.float32, kind="ExternalOutput").ap()
    hybrid_gated_parallel_block(nc, *args, out)
    r = _run(nc, [arrays], core_ids=[0])
    y = _np.asarray(r.results[0]["out_dram"])
    return _np.ascontiguousarray(y.transpose(1, 0, 2).reshape(KT * 128, SEQ).T)[None]
```

```python
from contextlib import ExitStack
import math

import concourse.bass as bass
from concourse import mybir

F32 = mybir.dt.float32
F32R = mybir.dt.float32r
I32 = mybir.dt.int32
U8 = mybir.dt.uint8
ACT = mybir.ActivationFunctionType
ALU = mybir.AluOpType
AX = mybir.AxisListType.X

LAYERS = 2
SEQ = 512
D_MODEL = 1024
KT = D_MODEL // 128
RW_W = 512
IN_COLS = 8704
IN_TILES = IN_COLS // 128
CONV_T0 = (1792 + 512) // 128
POOL_T0 = 1792 // 128
ATT_T0 = (1792 + 512 + 1536) // 128
GATE_T0 = ATT_T0 + 768 // 128
CONV_K = 3
POOL_WINDOWS = (2, 4, 8, 16)
HEADS = 8
WINDOW = 128
CHUNK = 64
D_FF = 2816
FT = D_FF // 128
NORM_EPS = 1e-6
LNX_EPS = 64e-5
ROPE_THETA = 10000.0
MASKED = -1e30
TT = SEQ // 128

CB = 4
RING = 4
BRANCH_ORDER = (2, 1, 3)
PROJ_TILES = GATE_T0
C_PROJ = PROJ_TILES * KT // CB
C_GROUP = (KT + 4) // CB
C_BRANCH = KT * C_GROUP
C_STEP = C_BRANCH // TT
C_SCAN = C_PROJ + 2 * C_BRANCH
C_BRANCH_B = C_PROJ + C_BRANCH
C_WO = C_SCAN + C_BRANCH
C_FFN = C_WO + KT * KT // CB
C_DOWN = C_FFN + 2 * FT * KT // CB
C_END = C_DOWN + KT * FT // CB
CHUNKS = C_END + C_BRANCH
BLOCKS = CHUNKS * CB
assert all(c % RING == 0 for c in (C_PROJ, C_BRANCH, C_SCAN, C_WO, C_FFN, C_DOWN, C_END))

ACCS = 4
T_JOINT = 2
T_PAIRS = T_JOINT + 24
T_KV = T_PAIRS + 8
assert T_KV + 2 == PROJ_TILES
T_MIX = PROJ_TILES
T_MIX_A = T_MIX + 2 * KT * 2
T_OUT_A = T_MIX_A + KT
T_WO = T_OUT_A + KT
T_FFN = T_WO + KT
T_DOWN = T_FFN + 2 * FT

_c = 0
COL = {}
for _n, _w in (("norm1", 8), ("norm2", 8), ("mu", 14), ("w0", 4), ("a0", 4), ("k_k", 4), ("k_a", 4), ("r_k", 4),
               ("lnx_g", 4), ("lnx_b", 4), ("pool_scale", 4), ("conv_w", 12), ("q_g", 1), ("k_g", 1), ("sinks", 8),
               ("lora_up", 512), ("g_up", 512), ("pool_w", 512)):
    COL[_n] = _c
    _c += _w
PARAM_COLS = _c
_c = 0
CON = {}
for _n, _w in (("eye", 128), ("same_head", 128), ("ones", 128), ("rot", 128), ("eye2", 64), ("corr", 64),
               ("bias_first", 256), ("bias", 256), ("inv_freq", 1)):
    CON[_n] = _c
    _c += _w
CONST_COLS = _c
_c = 0
MSK = {}
for _n, _w in (("upper", 128), ("upper_eq", 128), ("pair", 128), ("pair_t", 128), ("levels", 5 * 128), ("scan", SEQ)):
    MSK[_n] = _c
    _c += _w
MASK_COLS = _c


def hybrid_gated_parallel_block(nc, x_dram, pos_dram, w_dram, params_dram, consts_dram, masks_dram, out_dram):
    DECAY = math.exp(-0.5)
    scratch = nc.dram_tensor("scratch", (7, TT, 128, 4, 128), F32, kind="Internal").ap()
    x_keep = nc.dram_tensor("x_keep", (128, KT, SEQ), F32, kind="Internal").ap()
    SA, SR, SB, SK, SV, SG, SBON = range(7)

    with ExitStack() as ctx:
        at = [(nc.sbuf_base + 63) // 64 * 64]

        def place(name, shape, dt, offset=None):
            size = mybir.dt.size(dt)
            for n in shape[1:]:
                size *= n
            if offset is None:
                offset = at[0]
                at[0] += (size + 63) // 64 * 64
            assert offset + size <= nc.sbuf_usable_end, (name, offset + size)
            return nc.alloc_sbuf_tensor_at(name, list(shape), dt, offset=offset)

        xT = place("xT", [128, KT, SEQ], F32)
        yd_hi = place("yd_hi", [128, 4, SEQ], F32R, at[0] - KT * SEQ * 4)
        yd_lo = place("yd_lo", [128, 4, SEQ], F32R, at[0] - KT * SEQ * 2)
        consts = place("consts", [128, CONST_COLS], F32)
        masks = place("masks", [128, MASK_COLS], U8)
        params = place("params", [128, PARAM_COLS], F32)
        cosT = place("cosT", [128, SEQ], F32)
        sinT = place("sinT", [128, SEQ], F32)
        raw = place("raw", [128, RING, CB * 128], F32)
        w_hi = place("w_hi", [128, RING, CB * 128], F32R)
        w_lo = place("w_lo", [128, RING, CB * 128], F32R)
        h_hi = place("h_hi", [128, KT, SEQ], F32R)
        h_lo = place("h_lo", [128, KT, SEQ], F32R)
        sq2 = place("sq2", [128, 2, SEQ], F32, at[0] - 2 * SEQ * 4)
        sq_sum = place("sq_sum", [128, SEQ], F32, at[0] - 3 * SEQ * 4)
        mixed = place("mixed", [128, KT, SEQ], F32)
        state = place("state", [128, 2, 4, 64], F32)
        wc = place("wc", [128, 4, 8], F32)
        wcl = place("wcl", [128, 4, 2], F32)
        stat = place("stat", [128, 64], F32)
        one_minus_ka = place("one_minus_ka", [128, 4], F32)
        rstd = place("rstd", [128, SEQ], F32)
        U = at[0]
        KB = 1024
        workA = place("workA", [128, 32, 512], F32, U)
        y2_hi = place("y2_hi", [128, 2, 4, SEQ], F32R, U + 64 * KB)
        y2_lo = place("y2_lo", [128, 2, 4, SEQ], F32R, U + 80 * KB)
        yraw = place("yraw", [128, 4, SEQ], F32, U)
        workR = place("workR", [128, 44, 512], F32, U + 8 * KB)
        g_bonus = place("g_bonus", [128, 2, 4, SEQ], F32, U + 16 * KB)
        ya_hi = place("ya_hi", [128, 4, SEQ], F32R, U + 32 * KB)
        ya_lo = place("ya_lo", [128, 4, SEQ], F32R, U + 40 * KB)
        gate_a = place("gate_a", [128, KT, SEQ], F32, U + 48 * KB)
        tmpY = place("tmpY", [128, 4, 512], F32, U + 64 * KB)
        mx_hi = place("mx_hi", [128, KT, SEQ], F32R, U)
        mx_lo = place("mx_lo", [128, KT, SEQ], F32R, U + 16 * KB)
        tmpN = place("tmpN", [128, 2, 512], F32, U + 48 * KB)
        hid_hi = place("hid_hi", [128, FT, SEQ], F32R, U)
        hid_lo = place("hid_lo", [128, FT, SEQ], F32R, U + 44 * KB)
        tmpF = place("tmpF", [128, 4, 512], F32, U + 88 * KB)

        acc = [ctx.enter_context(nc.psum_tensor(f"acc{i}", [128, 512], F32)) for i in range(ACCS)]
        aux = [ctx.enter_context(nc.psum_tensor(f"aux{i}", [128, 512], F32)) for i in range(4)]

        def con(name, w=None):
            c = CON[name]
            return consts[:, c:c + (w or 128)]

        def msk(name, i=0, w=128):
            c = MSK[name] + i * w
            return masks[:, c:c + w]

        def par(name, i=0):
            c = COL[name] + i
            return params[:, c:c + 1]

        def mat(name, i=0):
            c = COL[name] + 128 * i
            return params[:, c:c + 128]

        def W(i, n=512, off=0):
            return workA[:, :, :].rearrange("p s n -> p (s n)")[:, i * 512 + off:i * 512 + off + n]

        def R(i, n=512):
            return workR[:, :, :].rearrange("p s n -> p (s n)")[:, i * 512:i * 512 + n]

        def sems(names, prefix=""):
            made = {n: ctx.enter_context(nc.semaphore(prefix + n)) for n in names.split()}
            nums = [s.num for s in made.values()]
            assert max(nums) - min(nums) == len(nums) - 1
            return made, range(min(nums), max(nums) + 1)

        setup, _ = sems("const_loaded masks_loaded x_loaded0 x_loaded1 x_loaded2 x_loaded3 pos_loaded out_stored setup_step angle_ready sq ssq var root rstd params_first raw_first", "setup_")
        L, layer_sems = sems(
            "x_kept x_back raw0 raw1 raw2 raw3 raw_ahead split_hi split_ready chunk_done acc_free "
            "h_full h_hi_ready h_ready sq sq_added ssq var root rstd first_done param_next "
            "first_operands gbonus_loaded ymean_mm yc_ready ysq_ready yvar_mm yvar_ready yroot_ready yfin_ready ya_hi_ready ya_ready "
            "vstep pad_ready astep praw_ready lora_in_ready lora_done sig_done g_done L_ready Lprev_ready E_done "
            "kksq_ready kkssq_done kk_clamped kk_root rk_ready rk_done staged "
            "st_A st_R st_B st_K st_V st_G st_bonus "
            "cs_ready y_full y_hi_ready y_ready pool_raw pool_mm qraw_ready qsq_ready qssq_done qvar_ready "
            "qroot_ready qn_ready rot_done qk_ready v_turned v_ready vpad_ready "
            "scores_done negmax_ready exp_done probs_ready turned pt_a pt_v pv_done yd_hi_ready yd_ready "
            "gate_sig mixed_ready mx_hi_ready mx_ready sig_ffn hid_hi_ready hid_ready")
        S, scan_sems = sems(
            "zeroed turned4 tokA_ready tokB_ready tokK_ready tokV_ready "
            "step_raw0 step_raw1 step_raw2 step_raw3 step_hi step_split step_chunk step_sig "
            "gramB gramB_ready m_ready gramK gramK_ready tkv_done tkv_ready "
            "lx lx_ready lm mt_ready ma_done nma_ready blk_ready blk2_ready reff_mm reff_ready pt_mm pt_ready q_mm q_ready wcl_ready "
            "s_mm s_ready y_mm y_read rstep x_zero next_ABKV next_R")

        class Step:

            def __init__(self, eng, sem):
                self.eng, self.sem, self.n = eng, sem, 0

            def __call__(self, ins, by=1):
                ins.then_inc(self.sem, by)
                self.n += by
                self.eng.wait_ge(self.sem, self.n)

        def last_chunk(tile):
            if tile < PROJ_TILES:
                return max(2 * tile + 2, 2 * ACCS)
            if T_MIX_A <= tile < T_OUT_A:
                return C_SCAN + 2 * (tile - T_MIX_A) + 2
            if T_OUT_A <= tile < T_WO:
                return C_SCAN + 2 * KT + (tile - T_OUT_A) + 1
            if tile < T_MIX_A:
                g, second = divmod(tile - T_MIX, 2)
                return C_PROJ + C_GROUP * g + 2 + second
            if tile < T_FFN:
                return C_WO + 2 * (tile - T_WO) + 2
            if tile < T_DOWN:
                return C_FFN + max(2 * (tile - T_FFN) + 2, 2 * ACCS)
            return C_DOWN + -(-(tile - T_DOWN + 1) * FT // CB)

        def square_act(act, i, k):
            if k >= 2:
                act.wait_ge(L["sq_added"], i * (KT - 2) + max(k - 2, 1))
            act.activation(sq2[:, k % 2, :], xT[:, k, :], ACT.Square).then_inc(L["sq"], 1)

        def add_square_dve(dve, i, k):
            dve.wait_ge(L["sq"], i * KT + k + 1)
            if k >= 2:
                dve.wait_ge(L["sq_added"], i * (KT - 2) + k - 1)
            dve.tensor_tensor(sq_sum[:, :], sq2[:, 0, :] if k == 1 else sq_sum[:, :], sq2[:, k % 2, :], ALU.add)\
                .then_inc(L["sq_added"], 1)

        def square_pe(pe, i):
            pe.wait_ge(L["sq_added"], (i + 1) * (KT - 2))
            pe.matmul(aux[0][:, :], con("ones"), sq_sum[:, :], start=True, stop=False)
            pe.wait_ge(L["sq"], (i + 1) * KT)
            pe.matmul(aux[0][:, :], con("ones"), sq2[:, (KT - 1) % 2, :], start=False, stop=True)\
                .then_inc(L["ssq"], 1)

        def root_act(act, D, i):
            act.wait_ge(D["var"], i + 1)
            act.activation(rstd[:, :], rstd[:, :], ACT.Sqrt).then_inc(D["root"], 1)

        def root_dve(dve, D, i):
            dve.wait_ge(D["ssq"], i + 1)
            dve.tensor_scalar(rstd[:, :], aux[0][:, :], 1.0 / D_MODEL, NORM_EPS, ALU.mult, ALU.add)\
                .then_inc(D["var"], 1)
            dve.wait_ge(D["root"], i + 1)
            dve.reciprocal(rstd[:, :], rstd[:, :]).then_inc(D["rstd"], 1)
            dve.wait_ge(D["rstd"], i + 1)

        def h_act(act, i, hf):
            for k in range(KT):
                act.wait_ge(L["h_full"], i * KT + k + 1)
                act.activation(h_hi[:, k, :], hf[k % 2], ACT.Copy).then_inc(L["h_hi_ready"], 1)

        def h_dve(dve, i, gain, hf):
            def low(k):
                dve.wait_ge(L["h_hi_ready"], i * KT + k + 1)
                dve.tensor_tensor(h_lo[:, k, :], hf[k % 2], h_hi[:, k, :].bitcast(F32), ALU.subtract)\
                    .then_inc(L["h_ready"], 1)

            for k in range(KT):
                if k >= 2:
                    dve.wait_ge(L["h_ready"], i * KT + k - 1)
                dve.scalar_tensor_tensor(hf[k % 2], xT[:, k, :], par(gain, k), rstd[:, :], ALU.mult, ALU.mult)\
                    .then_inc(L["h_full"], 1)
                if k >= 1:
                    low(k - 1)
            low(KT - 1)

        def first_tiles_pe(pe, chunk0, i):
            for k in range(KT):
                pe.wait_ge(L["split_ready"], chunk0 + k + 1)
                pe.wait_ge(L["h_ready"], i * KT + k + 1)
                hi, lo = h_rhs[k]
                for t in range(ACCS):
                    wh, wl = (w[:, k % RING, t * 128:t * 128 + 128] for w in (w_hi, w_lo))
                    pe.matmul(acc[t][:, :], wh, hi, start=(k == 0), stop=False)
                    pe.matmul(acc[t][:, :], wh, lo, start=False, stop=False)
                    mm = pe.matmul(acc[t][:, :], wl, hi, start=False, stop=(k == KT - 1))
                    if k == KT - 1 and t < ACCS - 1:
                        mm.then_inc(L["first_done"], 1)
                mm.then_inc(L["chunk_done"], 1)

        def blocks_pe(pe, bank, first, rhs, chunk0, slot0=0, ready=None):
            for k, (hi, lo) in enumerate(rhs):
                c, b = divmod(first + k, CB)
                slot = (slot0 + c) % RING
                if b == 0 or k == 0:
                    pe.wait_ge(L["split_ready"], chunk0 + (c + 1))
                if ready:
                    pe.wait_ge(ready, k + 1)
                wh, wl = (w[:, slot, b * 128:b * 128 + 128] for w in (w_hi, w_lo))
                pe.matmul(bank[:, :], wh, hi, start=(k == 0), stop=False)
                pe.matmul(bank[:, :], wh, lo, start=False, stop=False)
                mm = pe.matmul(bank[:, :], wl, hi, start=False, stop=(k == len(rhs) - 1))
                if b == CB - 1:
                    mm.then_inc(L["chunk_done"], 1)

        def tile_done(eng, tile):
            if tile < ACCS - 1:
                eng.wait_ge(L["first_done"], tile + 1)
            elif T_FFN <= tile < T_FFN + ACCS - 1:
                eng.wait_ge(L["first_done"], ACCS - 1 + tile - T_FFN + 1)
            else:
                eng.wait_ge(L["chunk_done"], last_chunk(tile))

        h_rhs = [(h_hi[:, k, :], h_lo[:, k, :]) for k in range(KT)]

        def group_act(act, n, tile, bank0, done, sg):
            act.wait_ge(L["chunk_done"], done)
            act.wait_ge(L["acc_free"], tile - 2)
            act.activation(sg, acc[bank0][:, :], ACT.Sigmoid).then_inc(L["gate_sig"], 1)

        def group_dve(dve, n, tile, bank0, done, sg, tmp, out, first):
            dve.wait_ge(L["chunk_done"], done)
            dve.wait_ge(L["gate_sig"], n)
            if not first and not (isinstance(n, int) and n == KT + 1):
                dve.wait_ge(L["mixed_ready"], n - (KT + 1))
            dve.tensor_tensor(out if first else tmp, sg, acc[bank0 + 1][:, :], ALU.mult).then_inc(L["acc_free"], 2)
            if not first:
                dve.wait_ge(L["acc_free"], tile + 2)
                dve.tensor_tensor(out, out, tmp, ALU.add).then_inc(L["mixed_ready"], 1)

        stream = w_dram

        def load_ahead(sp, first, slots, sem):
            for s in slots:
                sp.dma_start(raw[:, s, :], stream[bass.ds(first + s, 1)].rearrange("a p n -> (a p) n")).then_inc(sem(s), 16)

        def load_chunks(sp, first, c0, c1):
            with sp.Fori(c0 // RING, c1 // RING) as r:
                for s in range(RING):
                    sp.wait_ge(L["split_ready"], r * RING + (s - RING + 1))
                    sp.dma_start(raw[:, s, :], stream[bass.ds(r * RING + s + first, 1)].rearrange("a p n -> (a p) n"))\
                        .then_inc(L[f"raw{s}"], 16)

        def split_chunks(pool, c0, c1, parts):
            def split(s, loaded, free, done):
                if loaded is not None:
                    pool.wait_ge(L[f"raw{s}"], loaded)
                if free is not None:
                    pool.wait_ge(L["chunk_done"], free)
                pool.tensor_tensor(w_hi[:, s, :], raw[:, s, :], con("ones", 1).broadcast_to([128, CB * 128]), ALU.mult).then_inc(L["split_hi"], 1)
                pool.wait_ge(L["split_hi"], done)
                pool.tensor_tensor(w_lo[:, s, :], raw[:, s, :], w_hi[:, s, :].bitcast(F32), ALU.subtract)\
                    .then_inc(L["split_ready"], 1)

            for s in range(RING):
                split(s, None, c0 - RING + s + 1 if c0 else None, c0 + s + 1)
            with pool.Fori(c0 // RING + 1, c1 // RING) as r:
                for s in range(RING):
                    split(s, r * 16 + 16 * (1 - parts), r * RING + (s - RING + 1), r * RING + (s + 1))

        with nc.Block() as block:
            @block.sync
            def _(sp):
                sp.dma_start(W(0).bitcast(I32), pos_dram.rearrange("a s -> (a s)").partition_broadcast(128))\
                    .then_inc(setup["pos_loaded"], 16)
                sp.dma_start(consts[:, :], consts_dram).then_inc(setup["const_loaded"], 16)
                for k in range(0, KT, 2):
                    sp.dma_start(xT[:, k:k + 2, :], x_dram[:, k:k + 2, :]).then_inc(setup[f"x_loaded{k // 2}"], 16)
                sp.dma_start(W(6, MASK_COLS), masks_dram).then_inc(setup["masks_loaded"], 16)
                sp.dma_start(params[:, :], params_dram[0]).then_inc(setup["params_first"], 16)
                sp.dma_start(raw[:, :, :], stream[0:RING].rearrange("c p n -> p c n")).then_inc(setup["raw_first"], 16)
                sp.wait_ge(setup["params_first"], 16)
                sp.wait_ge(setup["raw_first"], 16)

            @block.tensor
            def _(pe):
                pe.wait_ge(setup["const_loaded"], 16)
                for k in range(KT):
                    pe.wait_ge(setup["sq"], k + 1)
                    mm = pe.matmul(aux[0][:, :], con("ones"), W(24 + k), start=(k == 0), stop=(k == KT - 1))
                mm.then_inc(setup["ssq"], 1)

            @block.vector
            def _(dve):
                step = Step(dve, setup["setup_step"])
                dve.wait_ge(setup["pos_loaded"], 16)
                step(dve.tensor_copy(W(1), W(0).bitcast(I32)))
                dve.wait_ge(setup["const_loaded"], 16)
                step(dve.tensor_scalar(W(2), W(1), consts[:, CON["inv_freq"]:CON["inv_freq"] + 1], None, ALU.mult))
                c1 = 6.28125
                c2 = float(int((2 * math.pi - c1) * 2 ** 21)) / 2 ** 21
                c3 = 2 * math.pi - c1 - c2
                big = 1.5 * 2.0 ** 23
                for i, shift in ((3, 0.0), (4, 0.25)):
                    step(dve.tensor_scalar(W(5), W(2), 1 / (2 * math.pi), shift, ALU.mult, ALU.add))
                    step(dve.tensor_scalar(W(5), W(5), big, None, ALU.add))
                    step(dve.tensor_scalar(W(5), W(5), -big, None, ALU.add))
                    step(dve.scalar_tensor_tensor(W(i), W(5), -c1, W(2), ALU.mult, ALU.add))
                    step(dve.scalar_tensor_tensor(W(i), W(5), -c2, W(i), ALU.mult, ALU.add))
                    step(dve.scalar_tensor_tensor(W(i), W(5), -c3, W(i), ALU.mult, ALU.add))
                    step(dve.tensor_scalar(W(i), W(i), shift * 2 * math.pi, math.pi, ALU.add, ALU.min))
                    dve.tensor_scalar(W(i), W(i), -math.pi, None, ALU.max).then_inc(setup["angle_ready"], 1)
                root_dve(dve, setup, 0)
                dve.wait_ge(setup["masks_loaded"], 16)
                dve.tensor_copy(masks[:, :], W(6, MASK_COLS))

            @block.scalar
            def _(act):
                for k in range(KT):
                    act.wait_ge(setup[f"x_loaded{k // 2}"], 16)
                    act.activation(W(24 + k), xT[:, k, :], ACT.Square).then_inc(setup["sq"], 1)
                root_act(act, setup, 0)
                act.wait_ge(setup["angle_ready"], 2)
                act.activation(sinT[:, :], W(3), ACT.Sin)
                act.activation(cosT[:, :], W(4), ACT.Sin)

        GB = R(0, 2048).rearrange("p (g j w t) -> p g j w t", g=2, j=4, w=2)
        GK = R(4, 2048).rearrange("p (g j w t) -> p g j w t", g=2, j=4, w=2)
        per_head = lambda i: R(i, 1024).rearrange("p (g j t) -> p g j t", g=2, j=4)
        M, MT, MAin, nMA = (per_head(i) for i in (8, 10, 14, 16))
        X = [per_head(12), per_head(38)]
        tok = lambda i: R(i).rearrange("p (j g c) -> p j g c", j=4, g=2)
        Btok, Ktok, Vtok = tok(18), tok(19), tok(20)
        blk = lambda i: R(i, 1024).rearrange("p (j g c n) -> p j g c n", j=4, g=2, c=2)
        Bblk, Vblk, nMTblk = blk(21), blk(23), blk(25)
        AR = R(27, 1024).rearrange("p (j w t) -> p j w t", j=4, w=2)
        feat = lambda i: R(i).rearrange("p (j t) -> p j t", j=4)
        Bf, Kf, Vf = (feat(i) for i in (29, 30, 31))
        sgS, tmpS = [R(32), R(33)], R(34)
        PT, Qs = (R(i).rearrange("p (j c n) -> p j c n", j=4, c=2) for i in (35, 36))
        decayed = R(37)
        R_eff = feat(40)
        rows = lambda g: slice(64 * g, 64 * g + 64)
        bank4 = lambda b: b[:, :].rearrange("p (j t) -> p j t", j=4)
        LEVELS = (2, 4, 8, 16, 32)

        def half(ap, l, second):
            return ap.rearrange("p j (b two n) -> p j b two n", two=2, n=LEVELS[l])[:, :, :, second, :]

        def half1(ap, l, second):
            return ap.rearrange("p (b two n) -> p b two n", two=2, n=LEVELS[l])[:, :, second, :]

        def packed(bank, l):
            return bank[:, 0:256].rearrange("p (j b n) -> p j b n", j=4, n=LEVELS[l])

        def load_operand(sp, row, a, sem):
            out = {SA: AR[:, :, 0, :], SR: AR[:, :, 1, :], SB: Bf, SK: Kf, SV: Vf}[a]
            blocks = scratch.rearrange("a t p j n -> (a t) p j n")
            sp.dma_start(out, blocks[bass.ds(row + a * TT, 1)].rearrange("a p j n -> (a p) j n")).then_inc(sem, 16)

        with nc.Fori(0, LAYERS) as layer:
            with nc.Block() as block:
                HF = [W(3), W(4)]
                LW, SGD = W(5), W(6)
                r_, k_, v_, d_ = W(7), W(8), W(9), W(10)
                sig_, L_, Lp_ = W(11), W(12), W(13)
                E1, E2, E3 = W(14), W(15), W(16)
                a_, kk_, g_ = W(17), W(18), W(19)
                kksq_, kkn_ = W(0), W(1)
                stA, stB, stK, bonus_, rk_ = W(2), W(3), W(4), W(12), W(13)
                praw = [W(20, 513, 513 * i) for i in range(3)]
                Cs, cu, ct = W(24), W(25, 514), W(27)
                yf = [W(28), W(29)]
                pbuf, q1, q2, zp = W(0, 528), W(5, 528), W(13, 528), [W(15), W(16)]
                qraw = [W(17), W(18), W(30)]
                qsq, qrst, qcos = W(19), W(12), W(31)
                Qf = [W(2), W(3), W(4), W(7)]
                kA, kB = W(20, 640), W(22, 640)
                vtok = W(8, 640).rearrange("p (s n) -> p s n", s=5)
                probs = [W(0, 1024), W(13, 1024)]
                pT = W(15, 1024)
                sgA, tmpA = [W(17), W(18)], W(19)
                shifted = [0, 1] + [T_JOINT + 6 * j + i for j in range(4) for i in range(3)]
                row_order = {0: 12, 1: 13} | {T_JOINT + 6 * j + i: 4 * i + j for j in range(4) for i in range(3)}

                @block.sync
                def _(sp):
                    sp.dma_start(x_keep, xT[:, :, :]).then_inc(L["x_kept"], 16)
                    first = layer * CHUNKS
                    load_chunks(sp, first, RING, C_BRANCH_B + 2 * RING)
                    for name in "ARBKV":
                        sp.wait_ge(L[f"st_{name}"], 4 * 16)
                    sp.wait_ge(L["qk_ready"], 5)
                    sp.wait_ge(L["chunk_done"], C_BRANCH_B)
                    for a in (SA, SR, SB, SK, SV):
                        load_operand(sp, 0, a, L["first_operands"])
                    load_chunks(sp, first, C_BRANCH_B + 2 * RING, C_SCAN)
                    sp.wait_ge(L["split_ready"], C_SCAN)
                    load_ahead(sp, first + C_SCAN, range(RING), lambda s: L["raw_ahead"])
                    sp.wait_ge(L["x_kept"], 16)
                    sp.wait_ge(L["first_operands"], 5 * 16)
                    sp.wait_ge(L["raw_ahead"], RING * 16)

                @block.gpsimd
                def _(pool):
                    split_chunks(pool, 0, C_SCAN, 1)

                @block.tensor
                def _(pe):
                    def proj(tile):
                        pe.wait_ge(L["acc_free"], tile - ACCS + 1)
                        blocks_pe(pe, acc[tile % ACCS], 0, h_rhs, 2 * tile, 2 * tile)

                    def lora(j):
                        if j == 0:
                            pe.wait_ge(L["lora_in_ready"], 2)
                            pe.wait_ge(L["acc_free"], 2)
                        else:
                            pe.wait_ge(L["staged"], 5 * j)
                            pe.wait_ge(L["sig_done"], 2 * j)
                            pe.wait_ge(L["g_done"], j)
                        up = mat("lora_up", j)
                        pe.matmul(aux[0][:, :], up[0:64], LW[0:64], start=True, stop=True).then_inc(L["lora_done"], 1)
                        pe.matmul(aux[1][:, :], up[64:128], LW[64:128], start=True, stop=True)\
                            .then_inc(L["lora_done"], 1)
                        pe.matmul(aux[2][:, :], mat("g_up", j), SGD, start=True, stop=True).then_inc(L["lora_done"], 1)

                    def kk_norm(j):
                        pe.wait_ge(L["kksq_ready"], j + 1)
                        if j >= 1:
                            pe.wait_ge(L["kk_clamped"], j)
                        pe.matmul(aux[3][:, :], con("same_head"), kksq_, start=True, stop=True)\
                            .then_inc(L["kkssq_done"], 1)

                    def rk_sum(j):
                        pe.wait_ge(L["rk_ready"], j + 1)
                        pe.matmul(aux[0][:, :], con("same_head"), rk_, start=True, stop=True).then_inc(L["rk_done"], 1)

                    first_tiles_pe(pe, 0, 0)
                    for j in range(4):
                        t = T_JOINT + 6 * j
                        for i in range(3):
                            if t + i >= ACCS:
                                proj(t + i)
                        lora(j)
                        proj(t + 3)
                        kk_norm(j)
                        proj(t + 4)
                        proj(t + 5)
                        rk_sum(j)

                    def pool_mm(g):
                        pe.wait_ge(L["acc_free"], T_PAIRS + 2 * g + 2)
                        if g == 0:
                            pe.wait_ge(L["staged"], 20)
                        if g >= 2:
                            pe.wait_ge(L["y_full"], 4 + g - 1)
                        pe.matmul(aux[g % 2][:, :], mat("pool_w", g), zp[g % 2], start=True, stop=True)\
                            .then_inc(L["pool_mm"], 1)

                    def q_ssq(i):
                        pe.wait_ge(L["qsq_ready"], i + 1)
                        pe.matmul(aux[2][:, :], con("same_head"), qsq, start=True, stop=True).then_inc(L["qssq_done"], 1)

                    def q_rot(i):
                        pe.wait_ge(L["qn_ready"], i + 1)
                        if i >= 1:
                            pe.wait_ge(L["qk_ready"], i)
                        pe.matmul(aux[3][:, :], con("rot"), qraw[i % 3], start=True, stop=True).then_inc(L["rot_done"], 1)

                    for i in range(4):
                        proj(T_PAIRS + 2 * i)
                        proj(T_PAIRS + 2 * i + 1)
                        if i >= 1:
                            q_rot(i - 1)
                            pool_mm(i - 1)
                        q_ssq(i)
                    proj(T_KV)
                    proj(T_KV + 1)
                    q_rot(3)
                    pool_mm(3)
                    q_ssq(4)

                    def gate(n):
                        tile = T_MIX + 2 * n
                        pe.wait_ge(L["acc_free"], tile - ACCS + 1)
                        blocks_pe(pe, acc[tile % ACCS], 0, h_rhs, C_PROJ + C_GROUP * n, C_GROUP * n % RING)

                    def output(n):
                        tile = T_MIX + 2 * n + 1
                        pe.wait_ge(L["acc_free"], tile - ACCS + 1)
                        if n % KT == 0:
                            pe.wait_ge(L["y_ready"], 4 * (n // KT + 1))
                        blocks_pe(pe, acc[tile % ACCS], KT, [(y2_hi[:, n // KT, k, :], y2_lo[:, n // KT, k, :])
                                                             for k in range(4)],
                                  C_PROJ + C_GROUP * n, C_GROUP * n % RING)

                    gate(0)
                    output(0)
                    q_rot(4)
                    pe.wait_ge(L["qraw_ready"], 6)
                    pe.wait_ge(L["y_full"], 7)
                    for b in range(TT):
                        mm = pe.transpose(aux[0][:, b * 128:b * 128 + 128], qraw[5 % 3][:, b * 128:b * 128 + 128],
                                          con("eye"))
                    mm.then_inc(L["v_turned"], 1)
                    gate(1)
                    pe.wait_ge(L["v_ready"], 1)
                    pe.wait_ge(L["vpad_ready"], 3)
                    pe.wait_ge(L["qk_ready"], 5)
                    pe.wait_ge(L["y_full"], 8)
                    for n in range(8):
                        b, jj = divmod(n, 2)
                        for tj in range(2):
                            for pr in range(2):
                                rows = slice(64 * pr, 64 * pr + 64)
                                keys = kA if pr == jj else kB
                                mm = pe.matmul(aux[pr][:, tj * 256:tj * 256 + 256],
                                               Qf[2 * jj + tj][rows, b * 128:b * 128 + 128],
                                               keys[rows, b * 128:b * 128 + 256], start=True, stop=True)
                        mm.then_inc(L["scores_done"], 1)
                        if n == 7:
                            gate(15)
                        output(2 * n + 1)
                        if n < 7:
                            gate(2 * n + 2)
                        pe.wait_ge(L["probs_ready"], n + 1)
                        if n >= 1:
                            pe.wait_ge(L["yd_ready"], n)
                        for pr in range(2):
                            for s in range(4):
                                mm = pe.transpose(aux[2 + pr][:, s * 128:s * 128 + 128],
                                                  probs[n % 2][:, pr * 512 + s * 128:pr * 512 + s * 128 + 128],
                                                  con("eye"))
                        mm.then_inc(L["turned"], 1)
                        if n < 7:
                            output(2 * n + 2)
                        if n < 6:
                            gate(2 * n + 3)
                        pe.wait_ge(L["pt_a"], n + 1)
                        pe.wait_ge(L["pt_v"], n + 1)
                        for pr in range(2):
                            for tj in range(2):
                                for blk in range(2):
                                    src = pr * 512 + tj * 256 + blk * 128
                                    mm = pe.matmul(aux[2][64 * pr:64 * pr + 64, tj * 128:tj * 128 + 128],
                                                   vtok[:, b + blk, 64 * jj:64 * jj + 64], pT[:, src:src + 128],
                                                   start=(blk == 0), stop=(blk == 1))
                        mm.then_inc(L["pv_done"], 1)

                @block.scalar
                def _(act):
                    h_act(act, 0, HF)

                    def done(tile):
                        tile_done(act, tile)

                    def shift_in(tile, n):
                        done(tile)
                        if n < 3:
                            act.wait_ge(L["vstep"], n + 2)
                        else:
                            act.wait_ge(L["acc_free"], shifted[n - 3] + 1)
                        act.activation(praw[n % 3][:, 1:513], acc[tile % ACCS][:, :], ACT.Copy)\
                            .then_inc(L["praw_ready"], 1)

                    def high(i):
                        act.wait_ge(L["y_full"], i + 1)
                        act.activation(y2_hi[:, i // 4, i % 4, :], yf[i % 2], ACT.Copy).then_inc(L["y_hi_ready"], 1)

                    def store(j):
                        act.wait_ge(L["staged"], 5 * (j + 1))
                        for a, src, name in ((SA, stA, "A"), (SR, r_, "R"), (SB, stB, "B"), (SK, stK, "K"),
                                             (SV, v_, "V"), (SG, g_, "G"), (SBON, bonus_, "bonus")):
                            act.dma_start(scratch[a][:, :, j, :].rearrange("t p n -> p t n"),
                                          src.rearrange("p (t n) -> p t n", t=TT)).then_inc(L[f"st_{name}"], 16)

                    shift_in(0, 0)
                    shift_in(1, 1)
                    act.wait_ge(L["acc_free"], 1)
                    act.activation(LW[0:64], LW[0:64], ACT.Tanh).then_inc(L["lora_in_ready"], 1)
                    act.wait_ge(L["acc_free"], 2)
                    act.activation(SGD, SGD, ACT.Sigmoid).then_inc(L["lora_in_ready"], 1)
                    for j in range(4):
                        t = T_JOINT + 6 * j
                        shift_in(t, 2 + 3 * j)
                        if j >= 1:
                            high(j - 1)
                        shift_in(t + 1, 3 + 3 * j)
                        shift_in(t + 2, 4 + 3 * j)
                        act.wait_ge(L["lora_done"], 3 * j + 1)
                        act.activation(sig_, aux[0][:, :], ACT.Sigmoid, bias=par("w0", j)).then_inc(L["sig_done"], 1)
                        act.wait_ge(L["lora_done"], 3 * j + 2)
                        act.activation(a_, aux[1][:, :], ACT.Sigmoid, bias=par("a0", j)).then_inc(L["sig_done"], 1)
                        act.wait_ge(L["lora_done"], 3 * j + 3)
                        if j >= 1:
                            act.wait_ge(L["st_G"], 16 * j)
                        act.activation(g_, aux[2][:, :], ACT.Copy).then_inc(L["g_done"], 1)
                        act.wait_ge(L["L_ready"], j + 1)
                        act.activation(E1, L_, ACT.Exp, scale=-DECAY).then_inc(L["E_done"], 1)
                        act.activation(E2, L_, ACT.Exp, scale=DECAY).then_inc(L["E_done"], 1)
                        act.wait_ge(L["Lprev_ready"], j + 1)
                        act.activation(E3, Lp_, ACT.Exp, scale=-DECAY).then_inc(L["E_done"], 1)
                        act.wait_ge(L["kk_clamped"], j + 1)
                        act.activation(kkn_, kkn_, ACT.Sqrt).then_inc(L["kk_root"], 1)
                        done(t + 3)
                        if j >= 1:
                            act.wait_ge(L["acc_free"], t - 1)
                        act.activation(Cs, acc[(t + 3) % ACCS][:, :], ACT.Copy).then_inc(L["cs_ready"], 1)
                        store(j)

                    def q_root(i):
                        act.wait_ge(L["qvar_ready"], i + 1)
                        act.activation(qrst, qrst, ACT.Sqrt).then_inc(L["qroot_ready"], 1)

                    def q_raw(i, tile):
                        done(tile)
                        if i >= 3:
                            act.wait_ge(L["qk_ready"], i - 2)
                        act.activation(qraw[i % 3], acc[tile % ACCS][:, :], ACT.Copy).then_inc(L["qraw_ready"], 1)

                    for i in range(4):
                        t = T_PAIRS + 2 * i
                        q_raw(i, t)
                        high(3 + i)
                        done(t + 1)
                        act.wait_ge(L["pad_ready"], 1)
                        if i >= 1:
                            act.wait_ge(L["acc_free"], t)
                        act.activation(pbuf[:, 16:528], acc[(t + 1) % ACCS][:, :], ACT.Copy).then_inc(L["pool_raw"], 1)
                        q_root(i)
                    q_raw(4, T_KV)
                    high(7)
                    q_raw(5, T_KV + 1)
                    q_root(4)

                    def gate(n):
                        t = T_MIX + 2 * n
                        group_act(act, n + 1, t, t % ACCS, last_chunk(t), sgA[n % 2])

                    act.wait_ge(L["qk_ready"], 4)
                    gate(0)
                    act.wait_ge(L["v_turned"], 1)
                    act.wait_ge(L["st_V"], 64)
                    act.activation(vtok[:, 1:5, :], aux[0][:, :].rearrange("p (s n) -> p s n", s=4), ACT.Copy)\
                        .then_inc(L["v_ready"], 1)
                    act.wait_ge(L["qk_ready"], 5)
                    gate(1)

                    for n in range(8):
                        b, jj = divmod(n, 2)
                        act.wait_ge(L["negmax_ready"], n + 1)
                        for s in range(4):
                            act.activation(probs[n % 2][:, s * 256:s * 256 + 256], probs[n % 2][:, s * 256:s * 256 + 256],
                                           ACT.Exp, bias=stat[:, 4 + s:5 + s], accum_out=stat[:, 8 + s:9 + s])\
                                .then_inc(L["exp_done"], 1)
                        act.activation(stat[:, 12:16], stat[:, 12:16], ACT.Exp).then_inc(L["exp_done"], 1)
                        gate(2 * n + 2 if n < 7 else 15)
                        act.wait_ge(L["turned"], n + 1)
                        if n >= 1:
                            act.wait_ge(L["pv_done"], n)
                        act.activation(pT[:, 0:512], aux[2][:, :], ACT.Copy).then_inc(L["pt_a"], 1)
                        if n < 6:
                            gate(2 * n + 3)
                        act.wait_ge(L["pv_done"], n + 1)
                        if n == 0:
                            act.wait_ge(L["x_kept"], 16)
                        act.activation(yd_hi[:, 2 * jj:2 * jj + 2, b * 128:b * 128 + 128],
                                       aux[2][:, 0:256].rearrange("p (t n) -> p t n", t=2), ACT.Copy)\
                            .then_inc(L["yd_hi_ready"], 1)
                    for name in ("A", "R", "B", "K", "V", "G", "bonus"):
                        act.wait_ge(L[f"st_{name}"], 64)

                @block.vector
                def _(dve):
                    step = Step(dve, L["vstep"])
                    free = Step(dve, L["acc_free"])
                    h_dve(dve, 0, "norm1", HF)
                    step(dve.memset(state[:, 0], 0.0))
                    for p in praw:
                        step(dve.memset(p[:, 0:1], 0.0))
                    step(dve.memset(cu[:, 0:2], 0.0))
                    step(dve.tensor_scalar(one_minus_ka[:, :], params[:, COL["k_a"]:COL["k_a"] + 4], -1.0, 1.0,
                                           ALU.mult, ALU.add))
                    def done(tile):
                        tile_done(dve, tile)

                    def mix(tile, n, out):
                        dve.wait_ge(L["praw_ready"], n + 1)
                        p = praw[n % 3]
                        step(dve.tensor_tensor(d_, p[:, 0:512], p[:, 1:513], ALU.subtract))
                        free(dve.scalar_tensor_tensor(out, d_, par("mu", row_order[tile]), p[:, 1:513],
                                                      ALU.mult, ALU.add))

                    def low(i):
                        dve.wait_ge(L["y_hi_ready"], i + 1)
                        dve.tensor_tensor(y2_lo[:, i // 4, i % 4, :], yf[i % 2],
                                          y2_hi[:, i // 4, i % 4, :].bitcast(F32), ALU.subtract)\
                            .then_inc(L["y_ready"], 1)

                    def conv_in(j):
                        t = T_JOINT + 6 * j + 3
                        done(t + 1)
                        dve.wait_ge(L["cs_ready"], j + 1)
                        free(dve.tensor_tensor(cu[:, 2:514], Cs, acc[(t + 1) % ACCS][:, :], ALU.mult), 2)

                    def conv_out(j):
                        t = T_JOINT + 6 * j + 3
                        step(dve.tensor_scalar(ct, cu[:, 0:512], par("conv_w", j), None, ALU.mult))
                        for tap in (1, 2):
                            step(dve.scalar_tensor_tensor(ct, cu[:, tap:tap + 512], par("conv_w", 4 * tap + j), ct,
                                                          ALU.mult, ALU.add))
                        done(t + 2)
                        if j >= 2:
                            dve.wait_ge(L["y_ready"], j - 1)
                        dve.tensor_tensor(yf[j % 2], ct, acc[(t + 2) % ACCS][:, :], ALU.mult).then_inc(L["y_full"], 1)
                        dve.wait_ge(L["y_full"], j + 1)
                        free(dve.memset(stat[:, 63:64], 0.0))
                        if j >= 1:
                            low(j - 1)

                    mix(0, 0, LW)
                    mix(1, 1, SGD)
                    for j in range(4):
                        if j >= 1:
                            dve.wait_ge(L["st_R"], 16 * j)
                            dve.wait_ge(L["st_V"], 16 * j)
                        for i, out in enumerate((r_, k_, v_)):
                            mix(T_JOINT + 6 * j + i, 2 + 3 * j + i, out)
                        dve.wait_ge(L["sig_done"], 2 * j + 1)
                        if j >= 1:
                            dve.wait_ge(L["st_bonus"], 16 * j)
                        dve.tensor_tensor_scan(L_, msk("scan", w=SEQ), sig_, 0.0, ALU.mult, ALU.add)\
                            .then_inc(L["L_ready"], 1)
                        dve.wait_ge(L["L_ready"], j + 1)
                        dve.tensor_tensor(Lp_, L_, sig_, ALU.subtract).then_inc(L["Lprev_ready"], 1)
                        step(dve.tensor_scalar(kk_, k_, par("k_k", j), None, ALU.mult))
                        dve.tensor_tensor(kksq_, kk_, kk_, ALU.mult).then_inc(L["kksq_ready"], 1)
                        dve.wait_ge(L["kkssq_done"], j + 1)
                        dve.tensor_scalar(kkn_, aux[3][:, :], 1e-24, None, ALU.max).then_inc(L["kk_clamped"], 1)
                        dve.wait_ge(L["kk_root"], j + 1)
                        step(dve.reciprocal(kkn_, kkn_))
                        step(dve.tensor_tensor(kk_, kk_, kkn_, ALU.mult))
                        dve.wait_ge(L["sig_done"], 2 * j + 2)
                        if j >= 1:
                            for name in ("A", "B", "K"):
                                dve.wait_ge(L[f"st_{name}"], 16 * j)
                        step(dve.tensor_tensor(stB, kk_, a_, ALU.mult))
                        dve.wait_ge(L["E_done"], 3 * j + 3)
                        dve.tensor_tensor(stB, stB, E2, ALU.mult).then_inc(L["staged"], 1)
                        dve.tensor_tensor(stA, kk_, E3, ALU.mult).then_inc(L["staged"], 1)
                        step(dve.tensor_scalar(a_, a_, par("k_a", j), one_minus_ka[:, j:j + 1], ALU.mult, ALU.add))
                        step(dve.tensor_tensor(k_, k_, a_, ALU.mult))
                        dve.tensor_tensor(stK, k_, E2, ALU.mult).then_inc(L["staged"], 1)
                        dve.scalar_tensor_tensor(rk_, r_, par("r_k", j), k_, ALU.mult, ALU.mult)\
                            .then_inc(L["rk_ready"], 1)
                        dve.wait_ge(L["rk_ready"], j + 1)
                        dve.tensor_tensor(r_, r_, E1, ALU.mult).then_inc(L["staged"], 1)
                        step(dve.tensor_copy(wc[:, j, :], E1.rearrange("p (c n) -> p c n", c=8)[:, :, CHUNK - 1]))
                        conv_in(j)
                        dve.wait_ge(L["rk_done"], j + 1)
                        dve.tensor_tensor(bonus_, aux[0][:, :], v_, ALU.mult).then_inc(L["staged"], 1)

                        conv_out(j)

                    def pool_out(g):
                        dve.wait_ge(L["pool_mm"], g + 1)
                        dve.wait_ge(L["y_ready"], 4 + g - 1)
                        dve.tensor_scalar(yf[g % 2], aux[g % 2][:, :], par("pool_scale", g), None, ALU.mult)\
                            .then_inc(L["y_full"], 1)
                        dve.wait_ge(L["y_full"], 4 + g + 1)

                    def pool_in(g):
                        win = POOL_WINDOWS[g]
                        dve.wait_ge(L["pool_raw"], g + 1)
                        src, dst, other, w = pbuf, q1, q2, 1
                        while w < win:
                            lo = 2 * w - 1
                            step(dve.tensor_tensor(dst[:, lo:528], src[:, lo:528], src[:, lo - w:528 - w], ALU.add))
                            src, dst, other = dst, other, dst
                            w *= 2
                        step(dve.tensor_tensor(src[:, 16:32], src[:, 16:32],
                                               consts[:, CON["corr"] + 16 * g:CON["corr"] + 16 * g + 16], ALU.mult))
                        if g >= 2:
                            dve.wait_ge(L["pool_mm"], g - 1)
                        free(dve.scalar_tensor_tensor(zp[g % 2], src[:, 16:528], 1.0 / win, pbuf[:, 16:528],
                                                      ALU.mult, ALU.subtract))

                    dve.memset(pbuf[:, 0:16], 0.0).then_inc(L["pad_ready"], 1)
                    for name in ("A", "B", "K", "R", "V", "G", "bonus"):
                        dve.wait_ge(L[f"st_{name}"], 64)
                    dve.memset(kA[:, 0:128], 0.0).then_inc(L["vpad_ready"], 1)
                    dve.memset(vtok[:, 0, :], 0.0).then_inc(L["vpad_ready"], 1)

                    def q_root(i):
                        dve.wait_ge(L["qssq_done"], i + 1)
                        dve.tensor_scalar(qrst, aux[2][:, :], 1.0 / 64, NORM_EPS, ALU.mult, ALU.add)\
                            .then_inc(L["qvar_ready"], 1)
                        dve.wait_ge(L["qroot_ready"], i + 1)
                        step(dve.reciprocal(qrst, qrst))
                        dve.scalar_tensor_tensor(qraw[i % 3], qraw[i % 3], par("q_g" if i < 4 else "k_g"), qrst,
                                                 ALU.mult, ALU.mult).then_inc(L["qn_ready"], 1)
                        dve.wait_ge(L["qn_ready"], i + 1)

                    def q_turn(i):
                        out = Qf[i] if i < 4 else kA[:, 128:640]
                        step(dve.tensor_tensor(qcos, qraw[i % 3], cosT[:, :], ALU.mult))
                        dve.wait_ge(L["rot_done"], i + 1)
                        step(dve.tensor_tensor(qrst, aux[3][:, :], sinT[:, :], ALU.mult))
                        dve.tensor_tensor(out, qcos, qrst, ALU.add).then_inc(L["qk_ready"], 1)
                        dve.wait_ge(L["qk_ready"], i + 1)

                    for i in range(6):
                        dve.wait_ge(L["qraw_ready"], i + 1)
                        if i < 5:
                            dve.tensor_tensor(qsq, qraw[i % 3], qraw[i % 3], ALU.mult).then_inc(L["qsq_ready"], 1)
                            dve.wait_ge(L["qsq_ready"], i + 1)
                        free(dve.memset(stat[:, 63:64], 0.0))
                        if 1 <= i < 5:
                            q_turn(i - 1)
                            pool_out(i - 1)
                        if i < 5:
                            low(3 + i)
                        if i < 4:
                            pool_in(i)
                            q_root(i)
                    q_root(4)
                    q_turn(4)
                    dve.wait_ge(L["vpad_ready"], 2)
                    step(dve.tensor_copy(kB[0:64, :], kA[64:128, :]))
                    dve.tensor_copy(kB[64:128, :], kA[0:64, :]).then_inc(L["vpad_ready"], 1)

                    def mix_in(n):
                        t = T_MIX + 2 * n
                        group_dve(dve, n + 1, t, t % ACCS, last_chunk(t + 1), sgA[n % 2], tmpA, mixed[:, n % 8, :],
                                  n < 8)

                    sinks = params[:, COL["sinks"]:COL["sinks"] + 8].rearrange("p (j q) -> p q j", q=2)
                    mix_in(0)
                    for n in range(8):
                        b, jj = divmod(n, 2)
                        P = probs[n % 2]
                        dve.wait_ge(L["scores_done"], n + 1)
                        bias = con("bias" if b else "bias_first", 256).unsqueeze(1).broadcast_to([128, 2, 256])
                        for pr in range(2):
                            step(dve.scalar_tensor_tensor(
                                P[:, pr * 512:pr * 512 + 512].rearrange("p (t n) -> p t n", t=2),
                                aux[pr][:, :].rearrange("p (t n) -> p t n", t=2), 0.125, bias, ALU.mult, ALU.add))
                        step(dve.tensor_reduce(stat[:, 0:4], P.rearrange("p (h n) -> p h n", h=4), AX, ALU.max))
                        sk = sinks[:, :, 2 * jj:2 * jj + 2]
                        m4 = stat[:, 0:4].rearrange("p (q t) -> p q t", q=2)
                        step(dve.tensor_tensor(m4, m4, sk, ALU.max))
                        step(dve.tensor_tensor(stat[:, 12:16].rearrange("p (q t) -> p q t", q=2), sk, m4, ALU.subtract))
                        dve.tensor_scalar(stat[:, 4:8], stat[:, 0:4], -1.0, None, ALU.mult)\
                            .then_inc(L["negmax_ready"], 1)
                        if n < 7:
                            mix_in(2 * n + 1)
                        dve.wait_ge(L["exp_done"], 5 * n + 5)
                        step(dve.tensor_tensor(stat[:, 8:12], stat[:, 8:12], stat[:, 12:16], ALU.add))
                        step(dve.reciprocal(stat[:, 8:12], stat[:, 8:12]))
                        p4 = P.rearrange("p (h n) -> p h n", h=4)
                        dve.tensor_tensor(p4, p4, stat[:, 8:12].unsqueeze(2).broadcast_to([128, 4, 256]), ALU.mult)\
                            .then_inc(L["probs_ready"], 1)
                        dve.wait_ge(L["turned"], n + 1)
                        if n >= 1:
                            dve.wait_ge(L["pv_done"], n)
                        dve.tensor_copy(pT[:, 512:1024], aux[3][:, :]).then_inc(L["pt_v"], 1)
                        mix_in(2 * n + 2 if n < 7 else 15)
                        dve.wait_ge(L["yd_hi_ready"], n + 1)
                        tok = slice(b * 128, b * 128 + 128)
                        dve.tensor_tensor(yd_lo[:, 2 * jj:2 * jj + 2, tok],
                                          aux[2][:, 0:256].rearrange("p (t n) -> p t n", t=2),
                                          yd_hi[:, 2 * jj:2 * jj + 2, tok].bitcast(F32), ALU.subtract)\
                            .then_inc(L["yd_ready"], 1)

            with nc.Fori(0, TT) as tt:
                with nc.Block() as block:
                    @block.sync
                    def _(sp):
                        for c in range(RING, C_STEP):
                            sp.wait_ge(S["step_split"], c - RING + 1)
                            sp.dma_start(raw[:, c % RING, :],
                                         stream[bass.ds(layer * CHUNKS + tt * C_STEP + (C_SCAN + c), 1)]
                                         .rearrange("a p n -> (a p) n")).then_inc(S[f"step_raw{c % RING}"], 16)
                        sp.wait_ge(S["gramK"], 4)
                        for a in (SA, SB, SK, SV):
                            load_operand(sp, tt + 1, a, S["next_ABKV"])
                        sp.wait_ge(S["reff_ready"], 1)
                        load_operand(sp, tt + 1, SR, S["next_R"])
                        sp.wait_ge(S["next_ABKV"], 4 * 16)
                        ahead = layer * CHUNKS + tt * C_STEP + (C_SCAN + C_STEP)
                        for s in (2, 3, 0, 1):
                            sp.wait_ge(S["step_split"], s + 1 if s >= C_STEP - RING else s + RING + 1)
                            load_ahead(sp, ahead, [s], lambda s: S[f"step_raw{s}"])
                        sp.wait_ge(S["next_R"], 16)
                        for s in range(RING):
                            sp.wait_ge(S[f"step_raw{s}"], 16 if s >= C_STEP - RING else 32)

                    @block.gpsimd
                    def _(pool):
                        def split(c):
                            s = c % RING
                            if c >= RING:
                                pool.wait_ge(S[f"step_raw{s}"], 16)
                                pool.wait_ge(S["step_chunk"], c - RING + 1)
                            pool.tensor_tensor(w_hi[:, s, :], raw[:, s, :], con("ones", 1).broadcast_to([128, CB * 128]),
                                               ALU.mult).then_inc(S["step_hi"], 1)
                            pool.wait_ge(S["step_hi"], c + 1)
                            pool.tensor_tensor(w_lo[:, s, :], raw[:, s, :], w_hi[:, s, :].bitcast(F32), ALU.subtract)\
                                .then_inc(S["step_split"], 1)

                        for c in range(RING):
                            split(c)
                        pool.wait_ge(S["step_split"], RING)
                        for t in (Bblk, Vblk, nMTblk):
                            pool.memset(t[0:64, :, :, 1, :], 0.0).then_inc(S["zeroed"], 1)
                            pool.memset(t[64:128, :, :, 0, :], 0.0).then_inc(S["zeroed"], 1)
                        pool.wait_ge(S["zeroed"], 6)
                        pool.wait_ge(S["tokB_ready"], 1)
                        for c in range(2):
                            pool.tensor_copy(Bblk[rows(c), :, :, c, :], Btok[rows(c)]).then_inc(S["blk_ready"], 1)
                        pool.wait_ge(S["tokV_ready"], 1)
                        for c in range(2):
                            pool.tensor_copy(Vblk[rows(c), :, :, c, :], Vtok[rows(c)]).then_inc(S["blk_ready"], 1)
                        pool.wait_ge(S["blk_ready"], 4)
                        for c in range(RING, C_STEP):
                            split(c)

                    @block.tensor
                    def _(pe):
                        filled = [0]

                        def fill(n):
                            for i in range(filled[0], filled[0] + n):
                                grp, k = divmod(i, 12)
                                c, b = divmod(i, CB)
                                if b == 0:
                                    pe.wait_ge(S["step_split"], c + 1)
                                bank = acc[2 * grp + (k >= KT)]
                                hi, lo = h_rhs[k] if k < KT else (yd_hi[:, k - KT, :], yd_lo[:, k - KT, :])
                                wh, wl = (w[:, c % RING, b * 128:b * 128 + 128] for w in (w_hi, w_lo))
                                pe.matmul(bank[:, :], wh, hi, start=(k in (0, KT)), stop=False)
                                pe.matmul(bank[:, :], wh, lo, start=False, stop=False)
                                mm = pe.matmul(bank[:, :], wl, hi, start=False, stop=(k in (KT - 1, KT + 3)))
                                if b == CB - 1:
                                    mm.then_inc(S["step_chunk"], 1)
                            filled[0] += n

                        for i, src in enumerate((AR[:, :, 0, :], Bf, Kf, Vf)):
                            for j in range(4):
                                mm = pe.transpose(bank4(aux[i])[:, j, :], src[:, j, :], con("eye"))
                            mm.then_inc(S["turned4"], 1)
                        free = ("tokA_ready", "tokB_ready", "tokK_ready", "tokV_ready")

                        def gram(src, sem, done):
                            for g in range(2):
                                for i in range(2):
                                    b = 2 * g + i
                                    done(b)
                                    for j in range(2 * i, 2 * i + 2):
                                        mm = pe.matmul(aux[b][:, (j % 2) * 256:(j % 2) * 256 + 256], src[rows(g), j, :],
                                                       AR[rows(g), j, :, :].rearrange("p w t -> p (w t)"),
                                                       start=True, stop=True)
                                    mm.then_inc(S[sem], 1)

                        gram(Bf, "gramB", lambda b: pe.wait_ge(S[free[b]], 1))
                        fill(2)
                        gram(Kf, "gramK", lambda b: pe.wait_ge(S["gramB_ready"], b + 1))
                        fill(4)
                        pe.wait_ge(S["gramK_ready"], 4)
                        for g in range(2):
                            for j in range(4):
                                mm = pe.matmul(aux[1][:, (4 * g + j) * 64:(4 * g + j) * 64 + 64], GK[:, g, j, 0, :],
                                               Vtok[:, j, g, :], start=True, stop=True)
                        mm.then_inc(S["tkv_done"], 1)
                        fill(1)
                        last = len(LEVELS) - 1
                        for l in range(len(LEVELS)):
                            for g in range(2):
                                pe.wait_ge(S["m_ready"], 2 * l + g + 1)
                                for j in range(4):
                                    mm = pe.matmul(packed(aux[2 * g], l)[:, j], GB[:, g, j, 0, :],
                                                   half1(M[:, g, j, :], l, 0), start=True, stop=True)
                                mm.then_inc(S["lx"], 1)
                            if l == 0:
                                pe.wait_ge(S["tkv_ready"], 1)
                            fill(1)
                            for g in range(2):
                                pe.wait_ge(S["lx_ready"], 2 * l + g + 1)
                                for j in range(4):
                                    mm = pe.matmul(packed(aux[2 * g + 1], l)[:, j], X[l % 2][:, g, j, :],
                                                   half1(MT[:, g, j, :], l, 1), start=True, stop=True)
                                mm.then_inc(S["lm"], 1)
                            fill(1)
                        fill(1)
                        for g in range(2):
                            pe.wait_ge(S["mt_ready"], 2 * last + g + 1)
                            for j in range(4):
                                mm = pe.matmul(bank4(aux[2 * g])[:, j, :], MT[:, g, j, :], MAin[:, g, j, :],
                                               start=True, stop=True)
                            mm.then_inc(S["ma_done"], 1)
                        fill(1)
                        pe.wait_ge(S["nma_ready"], 2)
                        pe.wait_ge(S["blk_ready"], 4)
                        for g in range(2):
                            for j in range(4):
                                mm = pe.matmul(bank4(aux[0])[rows(g), j, :], nMA[:, g, j, 0:64],
                                               Bblk[:, j, g].rearrange("p c n -> p (c n)"), start=True, stop=True)
                        mm.then_inc(S["pt_mm"], 1)
                        for g in range(2):
                            for j in range(4):
                                mm = pe.matmul(bank4(aux[1])[rows(g), j, :], nMA[:, g, j, 0:64], GB[:, g, j, 1, :],
                                               start=True, stop=True)
                        mm.then_inc(S["reff_mm"], 1)
                        fill(1)
                        pe.wait_ge(S["blk2_ready"], 4)
                        for g in range(2):
                            for j in range(4):
                                pe.matmul(bank4(aux[2])[rows(g), j, :], Ktok[:, j, g, :],
                                          Vblk[:, j, g].rearrange("p c n -> p (c n)"), start=True, stop=False)
                                mm = pe.matmul(bank4(aux[2])[rows(g), j, :], Btok[:, j, g, :],
                                               nMTblk[:, j, g].rearrange("p c n -> p (c n)"), start=False, stop=True)
                        mm.then_inc(S["q_mm"], 1)

                        def advance(c, bank):
                            for g in range(2):
                                for j in range(4):
                                    mm = pe.matmul(bank[rows(g), j * 64:j * 64 + 64], PT[rows(g), j, c, :],
                                                   state[rows(g), c, j, :], start=True, stop=True)
                            mm.then_inc(S["s_mm"], 1)

                        pe.wait_ge(S["pt_ready"], 1)
                        advance(0, aux[0])
                        pe.wait_ge(S["reff_ready"], 1)
                        fill(2)
                        pe.wait_ge(S["s_ready"], 1)
                        advance(1, aux[1])
                        fill(2)
                        for g in range(2):
                            for j in range(4):
                                out = bank4(aux[3])[rows(g), j, :]
                                pe.matmul(out, Vtok[:, j, g, :], GK[:, g, j, 1, :], start=True, stop=False)
                                pe.matmul(out, nMA[:, g, j, 64:128], GB[:, g, j, 1, :], start=False, stop=False)
                                for c in range(2):
                                    mm = pe.matmul(bank4(aux[3])[rows(g), j, 64 * c:64 * c + 64], state[rows(g), c, j, :],
                                                   R_eff[rows(g), j, 64 * c:64 * c + 64], start=False, stop=(c == 1))
                        mm.then_inc(S["y_mm"], 1)
                        assert filled[0] == C_STEP * CB

                    @block.scalar
                    def _(act):
                        def zero_x(l):
                            if l >= 2:
                                act.wait_ge(S["lm"], 2 * (l - 1))
                            act.activation(X[l % 2].rearrange("p g j t -> p (g j) t"),
                                           con("ones").unsqueeze(1).broadcast_to([128, 8, 128]), ACT.Copy, scale=0.0)\
                                .then_inc(S["x_zero"], 1)

                        act.wait_ge(S["turned4"], 1)
                        act.activation(MAin[:, :, :, 0:64].rearrange("p g j c -> p j g c"),
                                       aux[0][:, :].rearrange("p (j g c) -> p j g c", j=4, g=2), ACT.Copy)\
                            .then_inc(S["tokA_ready"], 1)
                        act.wait_ge(S["turned4"], 3)
                        act.activation(Ktok.rearrange("p j g c -> p (j g c)"), aux[2][:, :], ACT.Copy)\
                            .then_inc(S["tokK_ready"], 1)
                        zero_x(0)
                        zero_x(1)
                        act.wait_ge(S["tkv_done"], 1)
                        act.activation(MAin[:, :, :, 64:128], aux[1][:, :].rearrange("p (g j c) -> p g j c", g=2, j=4),
                                       ACT.Copy).then_inc(S["tkv_ready"], 1)
                        for l in range(2, len(LEVELS)):
                            zero_x(l)
                        act.wait_ge(S["step_chunk"], 2)
                        act.activation(sgS[0], acc[0][:, :], ACT.Sigmoid).then_inc(S["step_sig"], 1)
                        for g in range(2):
                            act.wait_ge(S["ma_done"], g + 1)
                            act.activation(nMA[:, g], bank4(aux[2 * g]), ACT.Copy, scale=-1.0).then_inc(S["nma_ready"], 1)
                        act.wait_ge(S["step_chunk"], 5)
                        act.activation(sgS[1], acc[2][:, :], ACT.Sigmoid).then_inc(S["step_sig"], 1)
                        act.wait_ge(S["y_mm"], 1)
                        act.activation(yraw[:, :, bass.ds(tt * 128, 128)], bank4(aux[3]), ACT.Copy)\
                            .then_inc(S["y_read"], 1)

                    @block.vector
                    def _(dve):
                        step = Step(dve, S["rstep"])
                        dve.wait_ge(S["turned4"], 2)
                        dve.tensor_copy(Btok.rearrange("p j g c -> p (j g c)"), aux[1][:, :]).then_inc(S["tokB_ready"], 1)
                        dve.wait_ge(S["turned4"], 4)
                        dve.tensor_copy(Vtok.rearrange("p j g c -> p (j g c)"), aux[3][:, :]).then_inc(S["tokV_ready"], 1)
                        dve.tensor_copy(wcl[:, :, :], wc[:, :, bass.ds(tt * 2, 2)]).then_inc(S["wcl_ready"], 1)
                        both = masks[:, MSK["upper"]:MSK["upper"] + 256].unsqueeze(1).broadcast_to([128, 2, 256])
                        four = lambda ap: ap.unsqueeze(1).broadcast_to([128, 4, 128])

                        def gram(out, sem, b):
                            g, i = divmod(b, 2)
                            dve.wait_ge(S[sem], b + 1)
                            dve.tensor_tensor(out[:, g, 2 * i:2 * i + 2].rearrange("p j w t -> p j (w t)"),
                                              aux[b][:, :].rearrange("p (j n) -> p j n", j=2), both, ALU.mult)\
                                .then_inc(S[sem + "_ready"], 1)

                        for b in range(4):
                            gram(GB, "gramB", b)
                        def turn(g):
                            dve.transpose(M[:, g].rearrange("p j t -> p (j t)"), MT[:, g].rearrange("p j t -> p (j t)"))\
                                .then_inc(S["m_ready"], 1)

                        for g in range(2):
                            dve.wait_ge(S["gramB_ready"], 2 * g + 2)
                            step(dve.tensor_tensor(MT[:, g], GB[:, g, :, 0, :], four(msk("pair_t")), ALU.mult))
                            step(dve.tensor_tensor(MT[:, g], four(con("eye")), MT[:, g], ALU.subtract))
                            turn(g)
                        for b in range(4):
                            gram(GK, "gramK", b)
                        for l in range(len(LEVELS)):
                            for g in range(2):
                                dve.wait_ge(S["lx"], 2 * l + g + 1)
                                dve.wait_ge(S["x_zero"], l + 1)
                                dve.tensor_tensor(half(X[l % 2][:, g], l, 0), packed(aux[2 * g], l),
                                                  half(four(msk("levels", l)), l, 0), ALU.mult)\
                                    .then_inc(S["lx_ready"], 1)
                            for g in range(2):
                                dve.wait_ge(S["lm"], 2 * l + g + 1)
                                dve.tensor_tensor(half(MT[:, g], l, 1), half(MT[:, g], l, 1), packed(aux[2 * g + 1], l),
                                                  ALU.subtract).then_inc(S["mt_ready"], 1)
                                if l < len(LEVELS) - 1:
                                    dve.wait_ge(S["mt_ready"], 2 * l + g + 1)
                                    turn(g)
                        mixed_out = lambda i: mixed[:, bass.ds(tt * 2 + i, 1), :].rearrange("p a n -> p (a n)")

                        def mix_in(i):
                            dve.wait_ge(S["step_sig"], i + 1)
                            dve.wait_ge(S["step_chunk"], 3 * i + 3)
                            step(dve.tensor_tensor(tmpS, sgS[i], acc[2 * i + 1][:, :], ALU.mult))
                            step(dve.tensor_tensor(mixed_out(i), mixed_out(i), tmpS, ALU.add))

                        dve.wait_ge(S["nma_ready"], 2)
                        dve.wait_ge(S["zeroed"], 6)
                        for c in range(2):
                            for g in range(2):
                                dve.tensor_copy(nMTblk[rows(c), :, g, c, :], nMA[rows(c), g, :, 64:128])\
                                    .then_inc(S["blk2_ready"], 1)
                        mix_in(0)
                        dve.wait_ge(S["pt_mm"], 1)
                        eye2 = con("eye2", 64).unsqueeze(1).broadcast_to([128, 8, 64])
                        dve.tensor_tensor(PT.rearrange("p j c n -> p (j c) n"),
                                          aux[0][:, :].rearrange("p (a n) -> p a n", a=8), eye2, ALU.add)\
                            .then_inc(S["pt_ready"], 1)
                        dve.wait_ge(S["reff_mm"], 1)
                        dve.tensor_tensor(R_eff, bank4(aux[1]), AR[:, :, 1, :], ALU.add)\
                            .then_inc(S["reff_ready"], 1)
                        dve.wait_ge(S["q_mm"], 1)
                        dve.wait_ge(S["wcl_ready"], 1)
                        w8 = wcl[:, :, :].rearrange("p j c -> p (j c)").unsqueeze(2).broadcast_to([128, 8, 64])
                        dve.tensor_tensor(Qs.rearrange("p j c n -> p (j c) n"),
                                          aux[2][:, :].rearrange("p (a n) -> p a n", a=8), w8, ALU.mult)\
                            .then_inc(S["q_ready"], 1)
                        dve.wait_ge(S["q_ready"], 1)
                        for c in range(2):
                            w4 = wcl[:, :, c].unsqueeze(2).broadcast_to([128, 4, 64])
                            dve.wait_ge(S["s_mm"], c + 1)
                            part = decayed[:, 256 * c:256 * c + 256].rearrange("p (j n) -> p j n", j=4)
                            step(dve.tensor_tensor(part, aux[c][:, 0:256].rearrange("p (j n) -> p j n", j=4), w4, ALU.mult))
                            if c == 1:
                                mix_in(1)
                                dve.wait_ge(S["y_mm"], 1)
                            dve.tensor_tensor(state[:, 1 - c], part, Qs[:, :, c, :], ALU.add).then_inc(S["s_ready"], 1)
                nc.all_engine_barrier(sems_to_clear=scan_sems)

            with nc.Block() as block:
                HF = [tmpN[:, 0, :], tmpN[:, 1, :]]
                sgF, tF = [tmpF[:, 0, :], tmpF[:, 1, :]], [tmpF[:, 2, :], tmpF[:, 3, :]]
                C_OUT_A = C_SCAN + 2 * KT
                GROUPS = 2 * KT

                @block.sync
                def _(sp):
                    for i, a in enumerate((SG, SBON)):
                        for t in range(TT):
                            sp.dma_start(g_bonus[:, i, :, t * 128:t * 128 + 128], scratch[a][t])\
                                .then_inc(L["gbonus_loaded"], 16)
                    first = layer * CHUNKS + C_BRANCH
                    load_chunks(sp, first, C_SCAN + RING, C_SCAN + 2 * RING)
                    sp.dma_start(xT[:, :, :], x_keep).then_inc(L["x_back"], 16)
                    load_chunks(sp, first, C_SCAN + 2 * RING, C_FFN + 4 * RING)
                    sp.wait_ge(L["h_ready"], 2 * KT)
                    sp.dma_start(params[:, :], params_dram[bass.ds(layer + 1, 1)].rearrange("a p n -> (a p) n"))\
                        .then_inc(L["param_next"], 16)
                    load_chunks(sp, first, C_FFN + 4 * RING, C_END)
                    sp.wait_ge(L["split_ready"], C_END)
                    load_ahead(sp, first + C_END, range(RING), lambda s: L["raw_ahead"])
                    sp.wait_ge(L["raw_ahead"], 2 * RING * 16)
                    sp.wait_ge(L["param_next"], 16)

                @block.gpsimd
                def _(pool):
                    split_chunks(pool, C_SCAN, C_END, 2)

                @block.tensor
                def _(pe):
                    def gate(m):
                        if m >= ACCS:
                            pe.wait_ge(L["gate_sig"], GROUPS + m - ACCS + 1)
                        blocks_pe(pe, acc[m % ACCS], 0, h_rhs, C_SCAN + 2 * m, 2 * m)

                    for j in range(4):
                        pe.matmul(aux[j][:, :], con("same_head"), yraw[:, j, :], start=True, stop=True)\
                            .then_inc(L["ymean_mm"], 1)
                    gate(0)
                    for j in range(4):
                        pe.wait_ge(L["ysq_ready"], j + 1)
                        pe.matmul(aux[j][:, :], con("same_head"), tmpY[:, j, :], start=True, stop=True)\
                            .then_inc(L["yvar_mm"], 1)
                    for m in range(1, KT):
                        gate(m)
                    for m in range(KT):
                        if m < ACCS:
                            pe.wait_ge(L["gate_sig"], GROUPS + ACCS + m + 1)
                        else:
                            pe.wait_ge(L["acc_free"], T_MIX_A + 2 * (m - ACCS + 1))
                        blocks_pe(pe, acc[m % ACCS], 0, [(ya_hi[:, k, :], ya_lo[:, k, :]) for k in range(4)],
                                  C_OUT_A + m, m, L["ya_ready"] if m == 0 else None)
                    for m in range(KT):
                        pe.wait_ge(L["acc_free"], T_WO + (m - ACCS + 1) * (2 if m < ACCS else 1))
                        blocks_pe(pe, acc[m % ACCS], 0, [(mx_hi[:, k, :], mx_lo[:, k, :]) for k in range(KT)],
                                  C_WO + 2 * m, 2 * m, L["mx_ready"] if m == 0 else None)
                    square_pe(pe, 0)
                    pe.wait_ge(L["acc_free"], T_FFN)
                    first_tiles_pe(pe, C_FFN, 1)
                    with pe.Fori(1, FT // 2) as it:
                        for i in range(4):
                            pe.wait_ge(L["acc_free"], it * 4 + (T_FFN + i - ACCS + 1))
                            blocks_pe(pe, acc[i], 0, h_rhs, it * 8 + (C_FFN + 2 * i), 2 * i)
                    for m in range(KT):
                        pe.wait_ge(L["acc_free"], T_DOWN + m - ACCS + 1)
                        blocks_pe(pe, acc[m % ACCS], m * FT, [(hid_hi[:, k, :], hid_lo[:, k, :]) for k in range(FT)],
                                  C_DOWN, 0, L["hid_ready"] if m == 0 else None)
                    square_pe(pe, 1)

                @block.scalar
                def _(act):
                    def gate(m):
                        act.wait_ge(L["chunk_done"], last_chunk(T_MIX_A + m))
                        act.activation(gate_a[:, m, :], acc[m % ACCS][:, :], ACT.Sigmoid).then_inc(L["gate_sig"], 1)

                    def high(j):
                        act.wait_ge(L["yfin_ready"], j + 1)
                        act.activation(ya_hi[:, j, :], yraw[:, j, :], ACT.Copy).then_inc(L["ya_hi_ready"], 1)

                    gate(0)
                    for j in range(4):
                        act.wait_ge(L["yvar_ready"], j + 1)
                        act.activation(tmpY[:, j, :], tmpY[:, j, :], ACT.Sqrt).then_inc(L["yroot_ready"], 1)
                    for m in range(1, KT):
                        gate(m)
                        if m in (3, 4):
                            high(2 * (m - 3))
                            high(2 * (m - 3) + 1)
                    act.wait_ge(L["ya_ready"], 4)
                    for m in range(KT):
                        act.wait_ge(L["mixed_ready"], KT + m + 1)
                        act.activation(mx_hi[:, m, :], mixed[:, m, :], ACT.Copy).then_inc(L["mx_hi_ready"], 1)
                    for m in range(KT):
                        act.wait_ge(L["acc_free"], T_WO + m + 1)
                        square_act(act, 0, m)
                    root_act(act, L, 0)
                    h_act(act, 1, HF)

                    def hidden(it, done):
                        for i in range(2):
                            done(i)
                            act.wait_ge(L["acc_free"], it * 4 + (T_FFN + 2 * i))
                            act.activation(sgF[i], acc[2 * i][:, :], ACT.Sigmoid).then_inc(L["sig_ffn"], 1)
                        for i in range(2):
                            act.wait_ge(L["acc_free"], it * 4 + (T_FFN + 2 * i + 2))
                            act.activation(hid_hi[:, bass.ds(it * 2 + i, 1), :].rearrange("p a n -> p (a n)"), tF[i],
                                           ACT.Copy).then_inc(L["hid_hi_ready"], 1)

                    hidden(0, lambda i: tile_done(act, T_FFN + 2 * i))
                    with act.Fori(1, FT // 2) as it:
                        hidden(it, lambda i: act.wait_ge(L["chunk_done"], it * 8 + (C_FFN + 4 * i + 2)))
                    for m in range(KT):
                        act.wait_ge(L["acc_free"], T_DOWN + m + 1)
                        square_act(act, 1, m)
                    root_act(act, L, 1)

                @block.vector
                def _(dve):
                    step = Step(dve, L["astep"])
                    for j in range(4):
                        y = yraw[:, j, :]
                        dve.wait_ge(L["ymean_mm"], j + 1)
                        dve.scalar_tensor_tensor(y, aux[j][:, :], -1.0 / 64, y, ALU.mult, ALU.add)\
                            .then_inc(L["yc_ready"], 1)
                        dve.wait_ge(L["yc_ready"], j + 1)
                        dve.tensor_tensor(tmpY[:, j, :], y, y, ALU.mult).then_inc(L["ysq_ready"], 1)
                    for j in range(4):
                        dve.wait_ge(L["yvar_mm"], j + 1)
                        dve.tensor_scalar(tmpY[:, j, :], aux[j][:, :], 1.0 / 64, LNX_EPS, ALU.mult, ALU.add)\
                            .then_inc(L["yvar_ready"], 1)
                    dve.wait_ge(L["gbonus_loaded"], 2 * TT * 16)
                    for j in range(4):
                        y, r = yraw[:, j, :], tmpY[:, j, :]
                        dve.wait_ge(L["yroot_ready"], j + 1)
                        step(dve.reciprocal(r, r))
                        step(dve.scalar_tensor_tensor(y, y, par("lnx_g", j), r, ALU.mult, ALU.mult))
                        step(dve.scalar_tensor_tensor(y, g_bonus[:, 1, j, :], par("lnx_b", j), y, ALU.add, ALU.add))
                        dve.tensor_tensor(y, y, g_bonus[:, 0, j, :], ALU.mult).then_inc(L["yfin_ready"], 1)
                    for j in range(4):
                        dve.wait_ge(L["ya_hi_ready"], j + 1)
                        dve.tensor_tensor(ya_lo[:, j, :], yraw[:, j, :], ya_hi[:, j, :].bitcast(F32), ALU.subtract)\
                            .then_inc(L["ya_ready"], 1)

                    def low(m):
                        dve.wait_ge(L["mx_hi_ready"], m + 1)
                        dve.tensor_tensor(mx_lo[:, m, :], mixed[:, m, :], mx_hi[:, m, :].bitcast(F32), ALU.subtract)\
                            .then_inc(L["mx_ready"], 1)

                    for m in range(KT):
                        dve.wait_ge(L["chunk_done"], last_chunk(T_OUT_A + m))
                        dve.wait_ge(L["gate_sig"], GROUPS + m + 1)
                        dve.tensor_tensor(gate_a[:, m, :], gate_a[:, m, :], acc[m % ACCS][:, :], ALU.mult)\
                            .then_inc(L["acc_free"], 2)
                        dve.wait_ge(L["acc_free"], T_MIX_A + 2 * m + 2)
                        dve.tensor_tensor(mixed[:, m, :], mixed[:, m, :], gate_a[:, m, :], ALU.add)\
                            .then_inc(L["mixed_ready"], 1)
                        if m >= 1:
                            low(m - 1)
                    low(KT - 1)
                    dve.wait_ge(L["x_back"], 16)
                    for m in range(KT):
                        if m >= 2:
                            add_square_dve(dve, 0, m - 1)
                        dve.wait_ge(L["chunk_done"], last_chunk(T_WO + m))
                        dve.tensor_tensor(xT[:, m, :], xT[:, m, :], acc[m % ACCS][:, :], ALU.add)\
                            .then_inc(L["acc_free"], 1)
                    root_dve(dve, L, 0)
                    dve.wait_ge(L["acc_free"], T_FFN)
                    h_dve(dve, 1, "norm2", HF)

                    def hidden(it, done):
                        for i in range(2):
                            dve.wait_ge(L["sig_ffn"], it * 2 + (i + 1))
                            dve.tensor_tensor(tF[i], sgF[i], acc[2 * i][:, :], ALU.mult).then_inc(L["acc_free"], 1)
                            dve.wait_ge(L["acc_free"], it * 4 + (T_FFN + 2 * i + 1))
                            done(i)
                            dve.tensor_tensor(tF[i], tF[i], acc[2 * i + 1][:, :], ALU.mult).then_inc(L["acc_free"], 1)
                        for i in range(2):
                            dve.wait_ge(L["hid_hi_ready"], it * 2 + (i + 1))
                            f = bass.ds(it * 2 + i, 1)
                            dve.tensor_tensor(hid_lo[:, f, :].rearrange("p a n -> p (a n)"), tF[i],
                                              hid_hi[:, f, :].rearrange("p a n -> p (a n)").bitcast(F32), ALU.subtract)\
                                .then_inc(L["hid_ready"], 1)
                        dve.wait_ge(L["hid_ready"], it * 2 + 2)

                    hidden(0, lambda i: tile_done(dve, T_FFN + 2 * i + 1))
                    with dve.Fori(1, FT // 2) as it:
                        hidden(it, lambda i: dve.wait_ge(L["chunk_done"], it * 8 + (C_FFN + 4 * i + 4)))
                    for m in range(KT):
                        if m >= 2:
                            add_square_dve(dve, 1, m - 1)
                        dve.wait_ge(L["chunk_done"], last_chunk(T_DOWN + m))
                        dve.tensor_tensor(xT[:, m, :], xT[:, m, :], acc[m % ACCS][:, :], ALU.add)\
                            .then_inc(L["acc_free"], 1)
                    root_dve(dve, L, 1)
            nc.all_engine_barrier(sems_to_clear=layer_sems)

        with nc.Block() as block:
            @block.sync
            def _(sp):
                sp.dma_start(out_dram, xT[:, :, :]).then_inc(setup["out_stored"], 16)
                sp.wait_ge(setup["out_stored"], 16)


def tile_blocks(w, rows, cols):
    L = w.shape[0]
    return w.reshape(L, rows, 128, cols, 128).transpose(0, 3, 1, 2, 4)


def weight_stream(inp):
    import numpy as np
    w_in = tile_blocks(inp["w_in"], KT, IN_TILES)
    order = [12, 13] + [i for j in range(4)
                        for i in (j, 4 + j, 8 + j, CONV_T0 + 4 + j, CONV_T0 + 8 + j, CONV_T0 + j)]
    order += [t for i in range(4) for t in (ATT_T0 + i, POOL_T0 + i)] + [ATT_T0 + 4, ATT_T0 + 5]
    abreast = lambda tiles: [np.stack([t[:, k] for t in tiles], axis=1) for k in range(KT)]
    parts = abreast([w_in[:, i] for i in order[:4]]) + [w_in[:, i] for i in order[4:]]
    outs = {b: tile_blocks(inp[n], 4, KT) for b, n in enumerate(("w_rwkv_out", "w_pool_out", "w_conv_out", "w_attn_out"))}
    groups = lambda b: [w for m in range(KT) for w in (w_in[:, GATE_T0 + KT * b + m], outs[b][:, m])]
    for b in BRANCH_ORDER:
        parts += groups(b)
    parts += [w_in[:, GATE_T0 + m] for m in range(KT)] + [outs[0][:, m] for m in range(KT)]
    w_o = tile_blocks(inp["w_o"], KT, KT)
    parts += [w_o[:, m] for m in range(KT)]
    gate, up = (tile_blocks(inp[n], KT, FT) for n in ("w_ffn_gate", "w_ffn_up"))
    ffn = [w for f in range(FT) for w in (gate[:, f], up[:, f])]
    parts += abreast(ffn[:4]) + ffn[4:]
    down = tile_blocks(inp["w_ffn_down"], FT, KT)
    parts += [down[:, m] for m in range(KT)]
    s = np.concatenate(parts, axis=1)
    L, n = s.shape[:2]
    assert n == BLOCKS
    chunks = np.ascontiguousarray(s.reshape(L, n // CB, CB, 128, 128).transpose(0, 1, 3, 2, 4)).reshape(L * n // CB, 128, CB * 128)
    return np.concatenate([chunks, chunks[:RING]])


def small_params(inp):
    import numpy as np
    L = inp["x"].shape[0] and inp["w_in"].shape[0]
    col = lambda v: v.reshape(L, -1, 128).transpose(0, 2, 1)
    twice = lambda v: np.concatenate([v, v], axis=1).reshape(L, 128, 1)
    cw = inp["conv_w"].reshape(L, CONV_K, 4, 128).transpose(0, 3, 1, 2).reshape(L, 128, CONV_K * 4)
    sinks = np.broadcast_to(inp["sinks"][:, None, :], (L, 128, HEADS))
    parts = [col(inp["norm1_g"]), col(inp["norm2_g"]), col(inp["shift_mu"]), col(inp["w0"]), col(inp["a0"]),
             col(inp["k_k"]), col(inp["k_a"]), col(inp["r_k"].reshape(L, -1)), col(inp["lnx_g"]), col(inp["lnx_b"]),
             col(inp["pool_scale"]), cw, twice(inp["q_norm_g"]), twice(inp["k_norm_g"]), sinks,
             np.concatenate([inp["w_decay_up"], inp["a_up"]], axis=1), inp["g_up"],
             inp["pool_w"].transpose(0, 2, 1, 3).reshape(L, 128, 512)]
    out = np.concatenate(parts, axis=2)
    assert out.shape[2] == PARAM_COLS
    return np.ascontiguousarray(out)


def constants():
    import numpy as np
    p = np.arange(128)
    row, col = p[:, None], p[None, :]
    same = row // CHUNK == col // CHUNK
    eye = (row == col)
    rot = np.where((col % 64 < 32) & (row == col + 32), -1.0, 0.0) + np.where((col % 64 >= 32) & (row == col - 32), 1.0, 0.0)
    eye2 = (row % 64 == np.arange(64)[None, :])
    t = np.arange(16)
    corr = np.concatenate([w / np.minimum(t + 1, w) for w in POOL_WINDOWS])[None, :].repeat(128, 0)
    key = np.arange(256)[None, :]
    dist = row + 128 - key
    band = (dist >= 0) & (dist < WINDOW)
    bias = [np.where(band & (key >= 128), 0.0, MASKED), np.where(band, 0.0, MASKED)]
    inv = (np.float32(ROPE_THETA) ** (-(p % 32).astype(np.float32) * np.float32(2.0) / np.float32(64)))[:, None]
    f = np.concatenate([eye, same, np.ones((128, 128)), rot, eye2, corr, *bias, inv], axis=1).astype(np.float32)
    levels = []
    for b in (2, 4, 8, 16, 32):
        levels.append((row // (2 * b) == col // (2 * b)) & (row // b > col // b))
    pair = (row // 2 == col // 2) & (row > col)
    scan = np.broadcast_to((np.arange(SEQ) % CHUNK != 0)[None, :], (128, SEQ))
    u = np.concatenate([same & (row < col), same & (row <= col), pair, pair.T, *levels, scan], axis=1).astype(np.float32)
    assert f.shape[1] == CONST_COLS and u.shape[1] == MASK_COLS
    return np.ascontiguousarray(f), np.ascontiguousarray(u)


def kernel(**inputs):
    import numpy as _np
    import concourse.bacc as _bacc
    from concourse import mybir as _mybir
    from concourse.bass_utils import run_bass_kernel_spmd as _run

    inp = {k: _np.asarray(v) for k, v in inputs.items()}
    f, u = constants()
    arrays = {
        "x_dram": _np.ascontiguousarray(inp["x"][0].T.reshape(KT, 128, SEQ).transpose(1, 0, 2)),
        "positions_dram": _np.ascontiguousarray(inp["positions"]),
        "weights_dram": weight_stream(inp),
        "params_dram": _np.concatenate([p := small_params(inp), p[:1]]),
        "consts_dram": f,
        "masks_dram": u,
    }
    nc = _bacc.Bacc("TRN2", target_bir_lowering=False, num_devices=1)
    args = [nc.dram_tensor(n, a.shape, _mybir.dt.from_np(a.dtype), kind="ExternalInput").ap() for n, a in arrays.items()]
    out = nc.dram_tensor("out_dram", (128, KT, SEQ), _mybir.dt.float32, kind="ExternalOutput").ap()
    hybrid_gated_parallel_block(nc, *args, out)
    r = _run(nc, [arrays], core_ids=[0])
    y = _np.asarray(r.results[0]["out_dram"])
    return _np.ascontiguousarray(y.transpose(1, 0, 2).reshape(KT * 128, SEQ).T)[None]
```
